# Optimizing a Trainium2 kernel written in Bass

```python
import jax, jax.numpy as jnp
from jax import lax
import numpy as np

D_MODEL = 2048
BATCH = 1
SEQ = 256
DEPTH = 1

LRU_WIDTH = D_MODEL // 2
LRU_BLOCKS = 8
LRU_BLOCK = LRU_WIDTH // LRU_BLOCKS
CONV_WIDTH = 4
LRU_C = 8.0
ATTN_HEAD_DIM = 64
ATTN_Q_HEADS = (D_MODEL - LRU_WIDTH) // ATTN_HEAD_DIM
ATTN_KV_HEADS = 2
ATTN_GROUP = ATTN_Q_HEADS // ATTN_KV_HEADS
WINDOW = 128
ATTN_BLOCK = 128
ROPE_THETA = 500000.0
ROPE_DIM = ATTN_HEAD_DIM // 4
Q_WIDTH = ATTN_Q_HEADS * ATTN_HEAD_DIM
KV_WIDTH = ATTN_KV_HEADS * ATTN_HEAD_DIM
MIX_IN = 2 * LRU_WIDTH + Q_WIDTH + 2 * KV_WIDTH
MIX_WIDTH = LRU_WIDTH + Q_WIDTH
PEER_HEADS = 8
PEER_N_KEYS = 128
PEER_N_EXPERTS = PEER_N_KEYS * PEER_N_KEYS
PEER_QUERY_DIM = 256
PEER_HALF = PEER_QUERY_DIM // 2
PEER_TOPK = 16
PEER_TOKEN_CHUNK = 128
NORM_EPS = 1e-6

kernel_name = 'hymba_rglru_swa_sink_peer_adaln'

def rms_norm(x, g):
    xf = x.astype(jnp.float32)
    y = xf * lax.rsqrt(jnp.mean(xf * xf, axis=-1, keepdims=True) + NORM_EPS)
    return (y * g.astype(jnp.float32)).astype(x.dtype)

def modulate(xn, shift, scale):
    return xn * (1.0 + scale[:, None, :]) + shift[:, None, :]

def partial_rope(t, positions):
    half = ROPE_DIM // 2
    inv_freq = jnp.power(ROPE_THETA, -2.0 * jnp.arange(half, dtype=jnp.float32) / ROPE_DIM)
    ang = positions.astype(jnp.float32)[..., None] * inv_freq
    cos = jnp.cos(ang)[:, :, None, :]
    sin = jnp.sin(ang)[:, :, None, :]
    rot = t[..., :ROPE_DIM].astype(jnp.float32)
    x1, x2 = rot[..., :half], rot[..., half:]
    rotated = jnp.concatenate([x1 * cos - x2 * sin, x2 * cos + x1 * sin], axis=-1)
    return jnp.concatenate([rotated.astype(t.dtype), t[..., ROPE_DIM:]], axis=-1)

def rg_lru_group(x_in, conv_w, conv_b, gate_a_w, gate_a_b, gate_x_w, gate_x_b, lam):
    B, S, _ = x_in.shape
    xp = jnp.pad(x_in, ((0, 0), (CONV_WIDTH - 1, 0), (0, 0)))
    xc = conv_b
    for k in range(CONV_WIDTH):
        xc = xc + conv_w[k] * xp[:, k:k + S]
    xb = xc.reshape(B, S, LRU_BLOCKS, LRU_BLOCK)
    r = jax.nn.sigmoid(jnp.einsum('bshi,hij->bshj', xb, gate_a_w).reshape(B, S, LRU_WIDTH) + gate_a_b)
    i = jax.nn.sigmoid(jnp.einsum('bshi,hij->bshj', xb, gate_x_w).reshape(B, S, LRU_WIDTH) + gate_x_b)
    log_a = -LRU_C * r.astype(jnp.float32) * jax.nn.softplus(-lam.astype(jnp.float32))
    a = jnp.exp(log_a)
    b = jnp.sqrt(-jnp.expm1(2.0 * log_a)) * (i * xc).astype(jnp.float32)

    def combine(left, right):
        a_l, b_l = left
        a_r, b_r = right
        return a_l * a_r, a_r * b_l + b_r

    _, h = lax.associative_scan(combine, (a, b), axis=1)
    return h.astype(x_in.dtype)

def sliding_window_attention(q, k, v, sinks):
    B, S, HQ, HD = q.shape
    nblk = S // ATTN_BLOCK
    qb = q.reshape(B, nblk, ATTN_BLOCK, ATTN_KV_HEADS, ATTN_GROUP, HD)

    def band(t):
        tp = jnp.pad(t, ((0, 0), (ATTN_BLOCK, 0), (0, 0), (0, 0)))
        tb = tp.reshape(B, nblk + 1, ATTN_BLOCK, ATTN_KV_HEADS, HD)
        return jnp.concatenate([tb[:, :-1], tb[:, 1:]], axis=2)

    kb, vb = band(k), band(v)
    scores = jnp.einsum('bnqhgd,bnkhd->bnhgqk', qb, kb).astype(jnp.float32) * (HD ** -0.5)
    q_i = jnp.arange(ATTN_BLOCK)[:, None]
    k_j = jnp.arange(2 * ATTN_BLOCK)[None, :]
    rel = q_i + ATTN_BLOCK - k_j
    key_pos = jnp.arange(nblk)[:, None, None] * ATTN_BLOCK + k_j[None] - ATTN_BLOCK
    valid = (rel >= 0) & (rel < WINDOW) & (key_pos >= 0)
    scores = jnp.where(valid[None, :, None, None], scores, -jnp.inf)
    sink = jnp.broadcast_to(sinks.astype(jnp.float32).reshape(1, 1, ATTN_KV_HEADS, ATTN_GROUP, 1, 1),
                            scores.shape[:-1] + (1,))
    probs = jax.nn.softmax(jnp.concatenate([scores, sink], axis=-1), axis=-1)[..., :-1]
    out = jnp.einsum('bnhgqk,bnkhd->bnqhgd', probs.astype(v.dtype), vb)
    return out.reshape(B, S, HQ * HD)

def peer_ffn(t, w_q, sub_keys, u_tab, v_tab):
    B, S, D = t.shape
    T = B * S
    tf = t.reshape(T, D)
    q = (tf @ w_q).reshape(T, PEER_HEADS, 2, PEER_HALF).astype(jnp.float32)
    s = jnp.einsum('thpd,hpnd->thpn', q, sub_keys.astype(jnp.float32))
    sv, si = lax.top_k(s, PEER_TOPK)
    cand_s = (sv[:, :, 0, :, None] + sv[:, :, 1, None, :]).reshape(T, PEER_HEADS, PEER_TOPK * PEER_TOPK)
    cand_i = (si[:, :, 0, :, None] * PEER_N_KEYS + si[:, :, 1, None, :]).reshape(T, PEER_HEADS, PEER_TOPK * PEER_TOPK)
    top_s, pos = lax.top_k(cand_s, PEER_TOPK)
    idx = jnp.take_along_axis(cand_i, pos, axis=-1)
    g = jax.nn.softmax(top_s, axis=-1)
    nch = T // PEER_TOKEN_CHUNK

    def expert_chunk(args):
        xc, ic, gc = args
        u = u_tab[ic]
        act = jax.nn.gelu(jnp.einsum('cd,chkd->chk', xc, u).astype(jnp.float32))
        w = (gc * act).astype(xc.dtype)
        return jnp.einsum('chk,chkd->cd', w, v_tab[ic])

    out = lax.map(expert_chunk, (tf.reshape(nch, PEER_TOKEN_CHUNK, D),
                                 idx.reshape(nch, PEER_TOKEN_CHUNK, PEER_HEADS, PEER_TOPK),
                                 g.reshape(nch, PEER_TOKEN_CHUNK, PEER_HEADS, PEER_TOPK)))
    return out.reshape(B, S, D)

def hybrid_layer(x, c, positions, w_ada, b_ada, norm1_g, w_in, conv_w, conv_b,
                 gate_a_w, gate_a_b, gate_x_w, gate_x_b, lam, q_norm_g, k_norm_g, sinks,
                 out_norm_lru_g, out_norm_attn_g, w_out, norm2_g, peer_w_q, peer_sub_keys,
                 peer_u, peer_v):
    B, S, _ = x.shape
    ada = jax.nn.silu(c) @ w_ada + b_ada
    sh1, sc1, g1, sh2, sc2, g2 = jnp.split(ada, 6, axis=-1)

    h = modulate(rms_norm(x, norm1_g), sh1, sc1)
    proj = h @ w_in
    splits = np.cumsum([LRU_WIDTH, LRU_WIDTH, Q_WIDTH, KV_WIDTH]).tolist()
    x_lru, y_lru, q, k, v = jnp.split(proj, splits, axis=-1)
    lru = rg_lru_group(x_lru, conv_w, conv_b, gate_a_w, gate_a_b, gate_x_w, gate_x_b, lam)
    lru = lru * jax.nn.gelu(y_lru)
    q = q.reshape(B, S, ATTN_Q_HEADS, ATTN_HEAD_DIM)
    k = k.reshape(B, S, ATTN_KV_HEADS, ATTN_HEAD_DIM)
    v = v.reshape(B, S, ATTN_KV_HEADS, ATTN_HEAD_DIM)
    q = partial_rope(rms_norm(q, q_norm_g), positions)
    k = partial_rope(rms_norm(k, k_norm_g), positions)
    attn = sliding_window_attention(q, k, v, sinks)
    mixed = jnp.concatenate([rms_norm(lru, out_norm_lru_g), rms_norm(attn, out_norm_attn_g)], axis=-1)
    x = x + g1[:, None, :] * (mixed @ w_out)

    h2 = modulate(rms_norm(x, norm2_g), sh2, sc2)
    x = x + g2[:, None, :] * peer_ffn(h2, peer_w_q, peer_sub_keys, peer_u, peer_v)
    return x

def setup_inputs(seed: int = 0) -> dict:
    key = jax.random.key(seed)
    ks = jax.random.split(key, 32)
    f32 = jnp.float32
    L, D = DEPTH, D_MODEL

    def nrm(k, shape, scale):
        return jax.random.normal(k, shape, f32) * scale

    def gain(k, shape):
        return 1.0 + 0.02 * jax.random.normal(k, shape, f32)

    a_c = jax.random.uniform(ks[10], (L, LRU_WIDTH), f32, minval=0.9, maxval=0.999)
    a0 = a_c ** (1.0 / LRU_C)
    lru_lambda = jnp.log(a0) - jnp.log1p(-a0)
    offsets = jax.random.randint(ks[3], (BATCH, 1), 0, 1024, dtype=jnp.int32)
    positions = offsets + jnp.arange(SEQ, dtype=jnp.int32)[None, :]
    return {
        'x': nrm(ks[0], (BATCH, SEQ, D), 1.0),
        'c': nrm(ks[1], (BATCH, D), 1.0),
        'positions': positions,
        'w_ada': nrm(ks[2], (L, D, 6 * D), 0.5 * D ** -0.5),
        'b_ada': nrm(ks[4], (L, 6 * D), 0.02),
        'norm1_g': gain(ks[5], (L, D)),
        'w_in': nrm(ks[6], (L, D, MIX_IN), D ** -0.5),
        'conv_w': nrm(ks[7], (L, CONV_WIDTH, LRU_WIDTH), CONV_WIDTH ** -0.5),
        'conv_b': nrm(ks[8], (L, LRU_WIDTH), 0.02),
        'lru_gate_a_w': nrm(ks[9], (L, LRU_BLOCKS, LRU_BLOCK, LRU_BLOCK), LRU_BLOCK ** -0.5),
        'lru_gate_a_b': nrm(ks[11], (L, LRU_WIDTH), 0.02),
        'lru_gate_x_w': nrm(ks[12], (L, LRU_BLOCKS, LRU_BLOCK, LRU_BLOCK), LRU_BLOCK ** -0.5),
        'lru_gate_x_b': nrm(ks[13], (L, LRU_WIDTH), 0.02),
        'lru_lambda': lru_lambda,
        'q_norm_g': gain(ks[14], (L, ATTN_HEAD_DIM)),
        'k_norm_g': gain(ks[15], (L, ATTN_HEAD_DIM)),
        'attn_sinks': nrm(ks[16], (L, ATTN_Q_HEADS), 0.5),
        'out_norm_lru_g': gain(ks[17], (L, LRU_WIDTH)),
        'out_norm_attn_g': gain(ks[18], (L, Q_WIDTH)),
        'w_out': nrm(ks[19], (L, MIX_WIDTH, D), MIX_WIDTH ** -0.5),
        'norm2_g': gain(ks[20], (L, D)),
        'peer_w_q': nrm(ks[21], (L, D, PEER_HEADS * PEER_QUERY_DIM), D ** -0.5),
        'peer_sub_keys': nrm(ks[22], (L, PEER_HEADS, 2, PEER_N_KEYS, PEER_HALF), PEER_HALF ** -0.5),
        'peer_u': nrm(ks[23], (L, PEER_N_EXPERTS, D), D ** -0.5),
        'peer_v': nrm(ks[24], (L, PEER_N_EXPERTS, D), PEER_HEADS ** -0.5),
    }

def reference(x, c, positions, w_ada, b_ada, norm1_g, w_in, conv_w, conv_b,
              lru_gate_a_w, lru_gate_a_b, lru_gate_x_w, lru_gate_x_b, lru_lambda,
              q_norm_g, k_norm_g, attn_sinks, out_norm_lru_g, out_norm_attn_g, w_out,
              norm2_g, peer_w_q, peer_sub_keys, peer_u, peer_v):
    for l in range(DEPTH):
        x = hybrid_layer(x, c, positions, w_ada[l], b_ada[l], norm1_g[l], w_in[l], conv_w[l], conv_b[l],
                         lru_gate_a_w[l], lru_gate_a_b[l], lru_gate_x_w[l], lru_gate_x_b[l], lru_lambda[l],
                         q_norm_g[l], k_norm_g[l], attn_sinks[l], out_norm_lru_g[l], out_norm_attn_g[l],
                         w_out[l], norm2_g[l], peer_w_q[l], peer_sub_keys[l], peer_u[l], peer_v[l])
    return x


_drawn_inputs = setup_inputs


def setup_inputs(seed=0):
    import zlib

    import numpy as np

    out = dict(_drawn_inputs(seed))
    spreads = {}
    factors = {'norm1_g': 7.362,
     'conv_b': 4.697,
     'lru_gate_a_b': 22.118,
     'lru_gate_x_b': 8.0,
     'q_norm_g': 8.0,
     'k_norm_g': 8.0,
     'attn_sinks': 64.0,
     'out_norm_lru_g': 8.0,
     'out_norm_attn_g': 8.0,
     'norm2_g': 7.071}
    for name, (base, spread) in spreads.items():
        noise = np.random.default_rng([zlib.crc32(name.encode()), seed]).standard_normal(out[name].shape)
        drawn = base * np.exp(spread * noise) if base else spread * noise
        out[name] = __import__('jax').numpy.asarray(drawn.astype(out[name].dtype))
    for name, factor in factors.items():
        out[name] = (out[name] * factor).astype(out[name].dtype)
    return out
```

```python
import math
from contextlib import ExitStack

import numpy as np

import concourse.bass as bass
from concourse import mybir

P = 128
D = 2048
TOK = 256
KC = D // P
TT = TOK // P
LRU = 1024
LC = LRU // P
HD = 64
NQ, NKV = 16, 2
NQK = NQ + NKV
QKV = (NQ + 2 * NKV) * HD
ROT = 8
ROPE_THETA = 500000.0
PH = 8
NKEY = 128
TOPK = 16
EPS = 1e-6
ADA_GROUPS = 6
SH1, SC1, G1, SH2, SC2, G2 = range(ADA_GROUPS)
NEG = -1e30
GONE = -3e38

RECTS = [(0, 1, 16), (1, 1, 8), (2, 2, 5), (4, 4, 3), (8, 8, 1)]
NCAND = sum(r * c for _, r, c in RECTS)

WSLOTS = 4
ASLOTS = 4
LATE_ASLOTS = 2
ROWS = 8
PAIR_ROWS = 2 * TT * 2 * TOPK

COLS = {}
_at = 0
for _name, _n in (("c", KC), ("b_ada", ADA_GROUPS * KC), ("norm1_g", KC), ("norm2_g", KC), ("out_g", KC),
                  ("conv_w", 4 * LC), ("conv_b", LC), ("gate_a_b", LC), ("gate_x_b", LC), ("lam", LC)):
    COLS[_name] = (_at, _at + _n)
    _at += _n
NCOLS = _at
NROWV = 2 * HD + NQ

ALU = mybir.AluOpType
ACT = mybir.ActivationFunctionType
AX = mybir.AxisListType.X
F32 = mybir.dt.float32
I32 = mybir.dt.int32
U32 = mybir.dt.uint32


class Chain:

    def __init__(self, engine, sem):
        self.engine, self.sem, self.count = engine, sem, 0

    def mark(self, ins):
        ins.then_inc(self.sem, 1)
        self.count += 1

    def settle(self):
        if self.count:
            self.engine.wait_ge(self.sem, self.count)

    def restart(self):
        self.settle()
        self.engine.sem_clear(self.sem)
        self.count = 0


def unit_heads(u):
    t, first, n = (0, 8 * u, 8) if u < 2 else (1, 4 * (u - 2), 4)
    heads = list(range(first, first + n, 2)) + list(range(first + 1, first + n, 2))
    return t, heads, P * (t + 1)


UNITS = 6
AFTER_CHUNK = {1: [("qk_transpose", 0)], 2: [("scores", 0)], 3: [("scores", 1), ("values", 0)],
               4: [("scores", 2), ("values", 1)], 5: [("scores", 3), ("values", 2)],
               6: [("scores", 4), ("values", 3)], 7: [("scores", 5), ("values", 4), ("values", 5)]}


def build(nc, xT, cols, rowv, pos, w_ada, b_gate2, w_qkv, w_chunks, gates, keys, peer_u, peer_v, out):
    with ExitStack() as ctx:
        def sb(name, shape, dt=F32):
            return ctx.enter_context(nc.sbuf_tensor(name, shape, dt))

        def sem(name):
            return ctx.enter_context(nc.semaphore(name))

        x2T = sb("x2T", [P, KC, TOK])
        hT = sb("hT", [P, KC, TOK])
        mixedT = sb("mixedT", [P, KC, TOK])
        h2tok = mixedT[:, :, :].rearrange("p a b -> p (a b)").rearrange("p (t d) -> p t d", t=TT)
        peer = sb("peer", [P, TT, D])
        w_ring = sb("w_ring", [P, WSLOTS, D])
        ada_ring = sb("ada_ring", [P, ASLOTS, D])
        ada_acc = sb("ada_acc", [P, 2, D])
        keysT = sb("keysT", [P, 2 * PH, NKEY])
        mixer = sb("mixer", [P, 6 * D])
        colv = sb("colv", [P, NCOLS])
        rows = sb("rows", [P, NROWV])
        ident = sb("ident", [P, P])
        ones = sb("ones", [P, P])
        small = sb("small", [P, 640])

        peer_flat = peer[:, :, :].rearrange("p t d -> p (t d)")
        gate_w = peer_flat[:, 0:2048].rearrange("p (g c n) -> p g c n", g=2, c=LC)
        qS = peer_flat[:, 2048:4096].rearrange("p (t q) -> p t q", t=TT)

        cut = [0]

        def part(n):
            cut[0] += n
            assert cut[0] <= 6 * D
            return mixer[:, cut[0] - n:cut[0]]

        kvS = part(512).rearrange("p (t n) -> p t n", t=TT)
        kdup = part(512).rearrange("p (t k u d) -> p t k u d", t=TT, k=NKV, u=2)
        qTr = part(2048).rearrange("p (t h n) -> p t h n", t=TT, h=8)
        kTr = part(512).rearrange("p (k n) -> p k n", k=NKV)
        probs = [part(8 * 129) for _ in range(2)]
        probsT = [part(1024) for _ in range(2)]
        qk_square = mixer[:, cut[0] - 2048 - 2 * 8 * 129:cut[0] - 2048 - 2 * 8 * 129 + NQK * HD]
        xpad = [part(260) for _ in range(2)]
        xconv = [part(TOK) for _ in range(2)]
        th_r = [part(TOK) for _ in range(2)]
        th_i = [part(TOK) for _ in range(2)]
        decay = [part(TOK) for _ in range(2)]
        drive = [part(TOK) for _ in range(2)]
        ysil = [part(TOK) for _ in range(2)]
        bscan = part(TOK)

        def ring_row(slot):
            if slot < 6:
                return mixer[:, slot * D:(slot + 1) * D]
            return ada_ring[:, LATE_ASLOTS + slot - 6, :]

        mask = [part(P), part(2 * P)]
        rinv = sb("rinv", [P, TOK])
        sqsum = sb("sqsum", [P, TOK])
        qpT = [sqsum, rinv]
        sqb = probs[0]

        at = [0]

        def little(n, dt=F32):
            at[0] += n
            assert at[0] <= 640
            v = small[:, at[0] - n:at[0]]
            return v if dt == F32 else v.bitcast(dt)

        silu_c = little(KC)
        ada_col = little(5 * KC).rearrange("p (g k) -> p g k", g=5)
        amp = little(KC)
        c4 = little(LC)
        half_ab = little(LC)
        half_xb = little(LC)
        angle = little(TT * ROT)
        turns = little(TT * ROT)
        sin_t = little(TT * ROT)
        cos_t = little(TT * ROT)
        invf = little(ROT)
        posf = little(TT)
        posi = little(TT, I32)
        qk_ms = little(NQK)
        mx = little(8)
        den = little(8)
        lam_t = [little(LC) for _ in range(4)]
        iota_c = little(NCAND)
        idx = [little(TT * TOPK, U32) for _ in range(2)]
        gsm = [little(TT * TOPK) for _ in range(2)]
        dots = little(TOPK)
        gel = little(TOPK)
        wgt = little(TOPK)
        tick = little(ROWS + 1)
        tksum = little(TT)

        tk = [0]

        def topk_part(n, dt=F32):
            tk[0] += n
            assert tk[0] <= D
            v = ada_acc[:, 0, tk[0] - n:tk[0]]
            return v if dt == F32 else v.bitcast(dt)

        sc_s = topk_part(2 * TT * NKEY)
        top_v = topk_part(2 * TT * TOPK).rearrange("p (a t k) -> p a t k", a=2, t=TT)
        top_i = topk_part(2 * TT * TOPK, U32).rearrange("p (a t k) -> p a t k", a=2, t=TT)
        top_f = topk_part(2 * TT * TOPK).rearrange("p (a t k) -> p a t k", a=2, t=TT)
        cand_s = topk_part(TT * NCAND).rearrange("p (t c) -> p t c", t=TT)
        cand_i = topk_part(TT * NCAND).rearrange("p (t c) -> p t c", t=TT)
        best_v = topk_part(TT * TOPK).rearrange("p (t k) -> p t k", t=TT)
        best_p = topk_part(TT * TOPK, U32).rearrange("p (t k) -> p t k", t=TT)
        best_e = topk_part(TT * TOPK).rearrange("p (t k) -> p t k", t=TT)
        best_f = topk_part(TT * TOPK).rearrange("p (t k) -> p t k", t=TT)
        hot = topk_part(TOPK * NCAND).rearrange("p (k c) -> p k c", k=TOPK)
        gate2 = ada_acc[:, 0, :]
        brow = w_ring[0:1, 0, :]

        bank = [ctx.enter_context(nc.psum_tensor(f"bank{i}", [P, 512], F32)) for i in range(8)]
        X_BANK, Y_BANK, GATE_BANK, EVEN_BANK, ODD_BANK, PT_BANK, ADA_BANK, STAT_BANK = range(8)

        s_cols, s_xin, s_rows, s_pos, s_gatew, s_keys, s_brow = map(
            sem, ("s_cols", "s_xin", "s_rows", "s_pos", "s_gatew", "s_keys", "s_brow"))
        s_w = [sem(f"s_w{i}") for i in range(WSLOTS)]
        s_w_used = sem("s_w_used")
        s_ada = [sem(f"s_ada{i}") for i in range(ASLOTS)]
        s_ada_late = [sem(f"s_ada_late{i}") for i in range(LATE_ASLOTS)]
        s_ada_used = sem("s_ada_used")
        s_const = sem("s_const")
        s_ones = sem("s_ones")
        s_dve, s_act = sem("s_dve"), sem("s_act")
        s_silu, s_cvec = sem("s_silu"), sem("s_cvec")
        s_sq1 = sem("s_sq1")
        s_stat, s_mean, s_root = sem("s_stat"), sem("s_mean"), sem("s_root")
        s_adaps, s_adacol = sem("s_adaps"), sem("s_adacol")
        s_scaled, s_h = sem("s_scaled"), sem("s_h")
        s_qkvps, s_qkvS = sem("s_qkvps"), sem("s_qkvS")
        s_ang, s_sin = sem("s_ang"), sem("s_sin")
        s_lamabs, s_lamexp, s_lam = sem("s_lamabs"), sem("s_lamexp"), sem("s_lam")
        s_qkms, s_qkroot, s_qk = sem("s_qkms"), sem("s_qkroot"), sem("s_qk")
        s_qkTps, s_qkT = sem("s_qkTps"), sem("s_qkT")
        s_xps, s_yps, s_gps = sem("s_xps"), sem("s_yps"), sem("s_gps")
        s_xev, s_conv, s_yev, s_gev = sem("s_xev"), sem("s_conv"), sem("s_yev"), sem("s_gev")
        s_decay, s_mag, s_sqrt, s_lru = sem("s_decay"), sem("s_mag"), sem("s_sqrt"), sem("s_lru")
        s_scps, s_scS, s_shift, s_exp, s_prob = (
            sem("s_scps"), sem("s_scS"), sem("s_shift"), sem("s_exp"), sem("s_prob"))
        s_PTps, s_PT, s_pvps, s_pv = sem("s_PTps"), sem("s_PT"), sem("s_pvps"), sem("s_pv")
        s_sqm, s_mix = sem("s_sqm"), sem("s_mix")
        s_ops, s_x2, s_x2sq, s_x2add = sem("s_ops"), sem("s_x2"), sem("s_x2sq"), sem("s_x2add")
        s_qps, s_qev, s_sps, s_sS = sem("s_qps"), sem("s_qev"), sem("s_sps"), sem("s_sS")
        s_h2ps, s_h2tok = sem("s_h2ps"), sem("s_h2tok")
        s_bests, s_bexp, s_idx = sem("s_bests"), sem("s_bexp"), sem("s_idx")
        s_row = [sem(f"s_row{i}") for i in range(ROWS)]
        s_row_used = sem("s_row_used")
        s_hold = sem("s_hold")
        s_gelu = sem("s_gelu")
        s_g2ps, s_g2 = sem("s_g2ps"), sem("s_g2")
        s_x2ps, s_fin, s_out = sem("s_x2ps"), sem("s_fin"), sem("s_out")

        def col(name, k=None):
            a, b = COLS[name]
            return colv[:, a:b] if k is None else colv[:, a + k:a + k + 1]

        q_gain, k_gain, sink = rows[:, 0:HD], rows[:, HD:2 * HD], rows[:, 2 * HD:2 * HD + NQ]

        def spread(ap, n, axis):
            wide = ap.unsqueeze(axis)
            shape = list(wide.shape)
            shape[axis] = n
            return wide.broadcast_to(shape)

        def piece(stack, n):
            return stack[bass.ds(n, 1)].rearrange("a p n -> (a p) n")

        block = ctx.enter_context(nc.Block())

        @block.sync
        def _(sp):
            sp.dma_start(colv[:, :], cols).then_inc(s_cols, 16)
            for j in range(ASLOTS):
                sp.dma_start(ada_ring[:, j, :], w_ada[j]).then_inc(s_ada[j], 16)
            sp.dma_start(x2T[:, :, :], xT.rearrange("p (k t) -> p k t", k=KC)).then_inc(s_xin, 16)
            sp.dma_start(rows[:, :], rowv).then_inc(s_rows, 16)
            sp.dma_start(posi, pos).then_inc(s_pos, 16)
            with sp.Fori(1, 2 * KC // ASLOTS) as i:
                for j in range(ASLOTS):
                    sp.wait_ge(s_ada_used, i * ASLOTS + j - ASLOTS + 3)
                    sp.dma_start(ada_ring[:, j, :], piece(w_ada, i * ASLOTS + j)).then_inc(s_ada[j], 16)
            for j in range(WSLOTS):
                sp.dma_start(w_ring[:, j, 0:QKV], w_qkv[j]).then_inc(s_w[j], 16)
            with sp.Fori(1, KC // WSLOTS) as i:
                for j in range(WSLOTS):
                    sp.wait_ge(s_w_used, i * WSLOTS + j - WSLOTS + 1)
                    sp.dma_start(w_ring[:, j, 0:QKV], piece(w_qkv, i * WSLOTS + j)).then_inc(s_w[j], 16)
            sp.dma_start(gate_w, gates.rearrange("p (g c n) -> p g c n", g=2, c=LC)).then_inc(s_gatew, 16)
            with sp.Fori(0, 4) as i:
                for j in range(12):
                    if j % 3 != 2:
                        w = j // 3 * 2 + j % 3
                        sp.wait_ge(s_w_used, KC + i * 8 + w - WSLOTS + 1)
                        sp.dma_start(w_ring[:, w % WSLOTS, :], piece(w_chunks, i * 8 + w)
                                     ).then_inc(s_w[w % WSLOTS], 16)
                    sp.wait_ge(s_ada_used, 2 * KC + i * 12 + j - ASLOTS + 3)
                    sp.dma_start(ada_ring[:, j % ASLOTS, :], piece(w_ada, 2 * KC + i * 12 + j)
                                 ).then_inc(s_ada[j % ASLOTS], 16)
            sp.dma_start(keysT[:, :, :], keys.rearrange("p (c n) -> p c n", c=2 * PH)).then_inc(s_keys, 16)
            with sp.Fori(0, 4) as i:
                for j in range(WSLOTS):
                    sp.wait_ge(s_w_used, 3 * KC + i * WSLOTS + j - WSLOTS + 1)
                    sp.dma_start(w_ring[:, j, :], piece(w_chunks, 2 * KC + i * WSLOTS + j)).then_inc(s_w[j], 16)
                for j in range(4):
                    sp.wait_ge(s_ada_used, 5 * KC + i * 4 + j - LATE_ASLOTS + 3)
                    sp.dma_start(ada_ring[:, j % LATE_ASLOTS, :], piece(w_ada, 5 * KC + i * 4 + j)
                                 ).then_inc(s_ada_late[j % LATE_ASLOTS], 16)
            sp.wait_ge(s_w_used, 4 * KC - WSLOTS + 1)
            sp.dma_start(brow, b_gate2).then_inc(s_brow, 16)
            for t in range(TT):
                sp.wait_ge(s_fin, 4 * (t + 1))
                sp.dma_start(out[t * P:(t + 1) * P, :], peer[:, t, :]).then_inc(s_out, 16)
            sp.wait_ge(s_out, 16 * TT)

        @block.gpsimd
        def _(pool):
            g = nc.gpsimd
            g.memset(ident[:, :], 0.0).then_inc(s_const, 1)
            g.memset(mask[0], 0.0).then_inc(s_const, 1)
            g.memset(mask[1], 0.0).then_inc(s_const, 1)
            g.memset(tick[:, ROWS:ROWS + 1], 0.0).then_inc(s_const, 1)
            g.memset(tick[:, 0:ROWS], 0.0).then_inc(s_hold, ROWS)
            g.iota(iota_c, pattern=[[1, NCAND]], base=0, channel_multiplier=0,
                   allow_small_or_imprecise_dtypes=True).then_inc(s_const, 1)
            pool.wait_ge(s_const, 5)
            g.affine_select(out=ident[:, :], in_=ident[:, :], compare_op=ALU.not_equal, fill=1.0, base=0,
                            pattern=[[-1, P]], channel_multiplier=1).then_inc(s_const, 1)
            g.affine_select(out=mask[0], in_=mask[0], compare_op=ALU.is_ge, fill=NEG, base=0,
                            pattern=[[-1, P]], channel_multiplier=1).then_inc(s_const, 1)
            g.affine_select(out=mask[1][:, 0:P], in_=mask[1][:, 0:P], compare_op=ALU.is_ge, fill=NEG, base=-1,
                            pattern=[[1, P]], channel_multiplier=-1).then_inc(s_const, 1)
            g.affine_select(out=mask[1][:, P:2 * P], in_=mask[1][:, P:2 * P], compare_op=ALU.is_ge, fill=NEG,
                            base=0, pattern=[[-1, P]], channel_multiplier=1).then_inc(s_const, 1)
            pool.wait_ge(s_mix, KC)
            g.memset(sqsum[:, :], 0.0).then_inc(s_x2add, WSLOTS)
            g.memset(peer[:, :, :], 0.0).then_inc(s_const, 1)
            with pool.Fori(0, KC // WSLOTS) as i:
                for j in range(WSLOTS):
                    pool.wait_ge(s_x2sq, i * WSLOTS + j + 1)
                    pool.wait_ge(s_x2add, i * WSLOTS + j + WSLOTS)
                    g.tensor_tensor(sqsum[:, :], sqsum[:, :], sqb[:, j * TOK:(j + 1) * TOK],
                                    ALU.add).then_inc(s_x2add, 1)
            with pool.Fori(0, PH // 2) as i:
                for local in range(PAIR_ROWS):
                    group, k = divmod(local, 2 * TOPK)
                    parity, t = divmod(group, TT)
                    table = peer_u if k < TOPK else peer_v
                    slot, c = local % ROWS, t * TOPK + k % TOPK
                    if local % (2 * TT * TOPK) == 0:
                        pool.wait_ge(s_idx, i * 2 + parity + 1)
                    pool.wait_ge(s_row_used, i * PAIR_ROWS + local + 1)
                    pool.wait_ge(s_hold, i * PAIR_ROWS + local + 1)
                    g.tensor_tensor(tick[:, slot:slot + 1], tick[:, ROWS:ROWS + 1], tick[:, ROWS:ROWS + 1],
                                    ALU.add).then_inc(s_hold, 1)
                    g.indirect_dma_start(ring_row(slot), None, table,
                                         bass.IndirectOffsetOnAxis(ap=idx[parity][:, c:c + 1], axis=0)
                                         ).then_inc(s_row[slot], 16)

        @block.tensor
        def _(pe):
            mm = nc.tensor.matmul

            def column_sums(g):
                pe.wait_ge(s_ada_used, 2 + (g + 1) * KC)
                if g:
                    pe.wait_ge(s_adacol, g)
                for k in range(KC):
                    last = mm(bank[ADA_BANK][:, k:k + 1], ada_acc[:, g % 2, k * P:(k + 1) * P], ones[:, 0:1],
                              start=True, stop=True)
                last.then_inc(s_adaps, 1)

            def token_sums(dst, parts):
                for k, sq in enumerate(parts):
                    last = mm(dst[:, 0:TOK], ones[:, :], sq, start=(k == 0), stop=(k == len(parts) - 1))
                last.then_inc(s_stat, 1)

            def weight_chunk(dst, slot, src, ready=None):
                for k in range(KC):
                    if ready is not None:
                        pe.wait_ge(ready[0], ready[1] + k + 1)
                    last = mm(dst[:, 0:TOK], w_ring[:, slot, k * P:(k + 1) * P], src[:, k, :],
                              start=(k == 0), stop=(k == KC - 1))
                last.then_inc(s_w_used, 1)

            pe.wait_ge(s_ones, 1)
            pe.wait_ge(s_sq1, 4)
            token_sums(bank[STAT_BANK], [mixedT[:, k, :] for k in range(KC)])
            column_sums(SH1)
            column_sums(SC1)

            for k in range(KC):
                pe.wait_ge(s_w[k % WSLOTS], 16 * (k // WSLOTS + 1))
                pe.wait_ge(s_h, k + 1)
                for t in range(TT):
                    for dst, a, b in ((2 * t, 0, 512), (2 * t + 1, 512, 1024), (4 + t, 1024, QKV)):
                        last = mm(bank[dst][:, 0:b - a], hT[:, k, t * P:(t + 1) * P], w_ring[:, k % WSLOTS, a:b],
                                  start=(k == 0), stop=(k == KC - 1))
                last.then_inc(s_w_used, 1)

            def qk_transpose(_):
                pe.wait_ge(s_qk, TT)
                pe.wait_ge(s_const, 9)
                for t in range(TT):
                    for pair in range(8):
                        dst = (EVEN_BANK, ODD_BANK, PT_BANK, STAT_BANK)[2 * t + pair // 4]
                        nc.tensor.transpose(bank[dst][:, pair % 4 * P:(pair % 4 + 1) * P],
                                            qS[:, t, pair * P:(pair + 1) * P], ident[:, :])
                for kv in range(NKV):
                    for t in range(TT):
                        at_ = (kv * TT + t) * P
                        last = nc.tensor.transpose(bank[ADA_BANK][:, at_:at_ + P],
                                                   kdup[:, t, kv, :, :].rearrange("p u d -> p (u d)"), ident[:, :])
                last.then_inc(s_qkTps, 1)

            def scores(u):
                t, heads, keys_n = unit_heads(u)
                pe.wait_ge(s_qkT, 5)
                if u:
                    pe.wait_ge(s_scS, 2 * u)
                for i, h in enumerate(heads):
                    o, at_ = h % 2, i % (len(heads) // 2) * keys_n
                    last = mm(bank[(EVEN_BANK, ODD_BANK)[o]][:, at_:at_ + keys_n],
                              qTr[o * HD:(o + 1) * HD, t, h // 2, :],
                              kTr[o * HD:(o + 1) * HD, h // (NQ // NKV), 0:keys_n], start=True, stop=True)
                last.then_inc(s_scps, 1)

            def values(u):
                t, heads, keys_n = unit_heads(u)
                nb = keys_n // P
                pr = probs[u % 2][:, 0:len(heads) * (keys_n + 1)].rearrange("p (h k) -> p h k", h=len(heads))
                pe.wait_ge(s_prob, u + 1)
                for b in range(8):
                    if u and b % 4 == 0:
                        pe.wait_ge(s_PT, 2 * (u - 1) + b // 4 + 1)
                    last = nc.tensor.transpose(bank[(PT_BANK, STAT_BANK)[b // 4]][:, b % 4 * P:(b % 4 + 1) * P],
                                               pr[:, b // nb, b % nb * P:(b % nb + 1) * P], ident[:, :])
                    if b % 4 == 3:
                        last.then_inc(s_PTps, 1)
                pe.wait_ge(s_PT, 2 * u + 2)
                if u:
                    pe.wait_ge(s_pv, u)
                for i, h in enumerate(heads):
                    o, pair, kv = h % 2, (h - heads[0]) // 2, h // (NQ // NKV)
                    for b in range(nb):
                        last = mm(bank[ADA_BANK][o * HD:(o + 1) * HD, pair * P:(pair + 1) * P],
                                  kvS[:, b, P + kv * HD:P + (kv + 1) * HD],
                                  probsT[u % 2][:, (i * nb + b) * P:(i * nb + b + 1) * P],
                                  start=(b == 0), stop=(b == nb - 1))
                last.then_inc(s_pvps, 1)

            steps = {"qk_transpose": qk_transpose, "scores": scores, "values": values}
            pe.wait_ge(s_qkvS, 6)
            for c in range(LC):
                n = KC + 2 * c
                pe.wait_ge(s_w[n % WSLOTS], 16 * (n // WSLOTS + 1))
                if c:
                    pe.wait_ge(s_xev, c)
                weight_chunk(bank[X_BANK], n % WSLOTS, hT)
                n += 1
                pe.wait_ge(s_w[n % WSLOTS], 16 * (n // WSLOTS + 1))
                if c:
                    pe.wait_ge(s_yev, c)
                weight_chunk(bank[Y_BANK], n % WSLOTS, hT)
                if c == 0:
                    pe.wait_ge(s_gatew, 16)
                pe.wait_ge(s_conv, c + 1)
                if c:
                    pe.wait_ge(s_gev, 2 * c)
                for gate in range(2):
                    last = mm(bank[GATE_BANK][:, gate * TOK:(gate + 1) * TOK], gate_w[:, gate, c, :],
                              xconv[c % 2], start=True, stop=True)
                last.then_inc(s_gps, 1)
                for step, u in AFTER_CHUNK.get(c, []):
                    steps[step](u)

            pe.wait_ge(s_sqm, 1)
            token_sums(bank[STAT_BANK], [hT[:, k, :] for k in range(LC)])
            pe.wait_ge(s_sqm, 2)
            token_sums(bank[PT_BANK], [hT[:, LC + k, :] for k in range(LC)])
            pe.wait_ge(s_pv, UNITS)
            column_sums(G1)

            pe.wait_ge(s_mix, KC)
            with pe.Fori(0, KC // WSLOTS) as i:
                for j in range(WSLOTS):
                    pe.wait_ge(s_w[j], i * 16 + 16 * (2 * KC // WSLOTS + 1))
                    pe.wait_ge(s_x2, i * WSLOTS + j + 1)
                    weight_chunk(bank[j], j, mixedT)
            column_sums(SH2)
            column_sums(SC2)
            pe.wait_ge(s_x2add, WSLOTS + KC)
            token_sums(bank[STAT_BANK], [sqsum[:, :]])

            def peer_scores(i, parity):
                head = i * 2 + parity
                first = isinstance(head, int) and head == 0
                for half in range(2):
                    slot = 2 * parity + half
                    pe.wait_ge(s_w[slot], i * 16 + 16 * (3 * KC // WSLOTS + 1))
                    if not first:
                        pe.wait_ge(s_qev, head * 2 + half - 1)
                    weight_chunk(bank[half], slot, hT, (s_h, KC) if first and half == 0 else None)
                if first:
                    pe.wait_ge(s_keys, 16)
                else:
                    pe.wait_ge(s_bests, head)
                for half in range(2):
                    pe.wait_ge(s_qev, head * 2 + half + 1)
                    kt = (keysT[:, half, :] if first else
                          keysT[:, bass.ds(head * 2 + half, 1), :].rearrange("p a n -> p (a n)"))
                    for t in range(TT):
                        at_ = (half * TT + t) * P
                        last = mm(bank[2][:, at_:at_ + P], qpT[half][:, t * P:(t + 1) * P], kt,
                                  start=True, stop=True)
                last.then_inc(s_sps, 1)

            peer_scores(0, 0)
            for n in range(TT * 4):
                t, quarter = divmod(n, 4)
                dst = bank[(3, 4, 5, 7)[n % 4]]
                if n >= 4:
                    pe.wait_ge(s_h2tok, n - 3)
                for k in range(4):
                    last = nc.tensor.transpose(dst[:, k * P:(k + 1) * P],
                                               hT[:, quarter * 4 + k, t * P:(t + 1) * P], ident[:, :])
                last.then_inc(s_h2ps, 1)
            peer_scores(0, 1)
            with pe.Fori(1, PH // 2) as i:
                peer_scores(i, 0)
                peer_scores(i, 1)

            pe.wait_ge(s_ada_used, 2 + ADA_GROUPS * KC)
            pe.wait_ge(s_brow, 16)
            for n in range(4):
                dst = bank[3 + n]
                mm(dst[:, :], ones[:, :], ada_acc[:, 1, n * 512:(n + 1) * 512], start=True, stop=False)
                mm(dst[:, :], ones[0:1, :], brow[:, n * 512:(n + 1) * 512], start=False, stop=True
                   ).then_inc(s_g2ps, 1)
            pe.wait_ge(s_bests, PH)
            for t in range(TT):
                if t:
                    pe.wait_ge(s_g2, 4)
                for n in range(4):
                    dst = bank[((0, 1, 2, 7), (3, 4, 5, 6))[t][n]]
                    for k in range(4):
                        last = nc.tensor.transpose(dst[:, k * P:(k + 1) * P],
                                                   x2T[:, n * 4 + k, t * P:(t + 1) * P], ident[:, :])
                    last.then_inc(s_x2ps, 1)

        @block.scalar
        def _(act):
            fn = nc.scalar.activation
            own = Chain(act, s_act)
            act.wait_ge(s_cols, 16)
            fn(amp, col("c"), ACT.Tanh, scale=0.5).then_inc(s_silu, 1)
            own.mark(fn(lam_t[0], col("lam"), ACT.Abs))
            own.settle()
            fn(lam_t[0], lam_t[0], ACT.Exp, scale=-1.0).then_inc(s_lamexp, 1)
            act.wait_ge(s_xin, 16)
            for q in range(4):
                fn(mixedT[:, 4 * q:4 * q + 4, :], x2T[:, 4 * q:4 * q + 4, :], ACT.Square).then_inc(s_sq1, 1)
            act.wait_ge(s_ang, 1)
            fn(sin_t, angle, ACT.Sin).then_inc(s_sin, 1)
            fn(cos_t, angle, ACT.Sin, scale=0.5).then_inc(s_sin, 1)

            roots = [0]

            def root(v):
                roots[0] += 1
                act.wait_ge(s_mean, roots[0])
                fn(v, v, ACT.Sqrt).then_inc(s_root, 1)

            def shift(g, base):
                with act.Fori(0, KC) as k:
                    act.wait_ge(s_scaled, k + base + 1)
                    v = hT[:, bass.ds(k, 1), :]
                    fn(v, v, ACT.Identity, bias=ada_col[:, g, bass.ds(k, 1)]).then_inc(s_h, 1)

            root(rinv[:, :])
            act.wait_ge(s_adacol, 1)
            shift(SH1, 0)

            act.wait_ge(s_w_used, KC)
            for t in range(TT):
                for b, dst in ((2 * t, qS[:, t, 0:512]), (2 * t + 1, qS[:, t, 512:1024]), (4 + t, kvS[:, t, :])):
                    fn(dst, bank[b][:, 0:dst.shape[-1]], ACT.Copy).then_inc(s_qkvS, 1)

            def qk_transpose(_):
                act.wait_ge(s_qkTps, 1)
                for n, b in enumerate((EVEN_BANK, ODD_BANK, PT_BANK, STAT_BANK)):
                    fn(qTr[:, n // 2, n % 2 * 4:n % 2 * 4 + 4, :], bank[b][:, :].rearrange("p (h n) -> p h n", h=4),
                       ACT.Copy).then_inc(s_qkT, 1)
                fn(kTr, bank[ADA_BANK][:, :].rearrange("p (k n) -> p k n", k=NKV), ACT.Copy).then_inc(s_qkT, 1)

            def scores(u):
                _, heads, keys_n = unit_heads(u)
                act.wait_ge(s_shift, u + 1)
                v = probs[u % 2][:, 0:len(heads) * (keys_n + 1)]
                fn(v, v, ACT.Exp).then_inc(s_exp, 1)

            def values(u):
                t, heads, _ = unit_heads(u)
                for b in range(2):
                    act.wait_ge(s_PTps, 2 * u + b + 1)
                    if u >= 2 and b == 0:
                        act.wait_ge(s_pvps, u - 1)
                    fn(probsT[u % 2][:, b * 512:(b + 1) * 512], bank[(PT_BANK, STAT_BANK)[b]][:, :],
                       ACT.Copy).then_inc(s_PT, 1)
                act.wait_ge(s_pvps, u + 1)
                pairs, first = len(heads) // 2, heads[0] // 2
                fn(mixedT[:, LC + first:LC + first + pairs, t * P:(t + 1) * P],
                   bank[ADA_BANK][:, 0:pairs * P].rearrange("p (h n) -> p h n", h=pairs),
                   ACT.Copy).then_inc(s_pv, 1)

            steps = {"qk_transpose": qk_transpose, "scores": scores, "values": values}
            for c in range(LC):
                b = c % 2
                act.wait_ge(s_w_used, KC + 2 * c + 1)
                if c >= 2:
                    act.wait_ge(s_conv, c - 1)
                elif c == 0:
                    act.wait_ge(s_const, 9)
                fn(xpad[b][:, 3:3 + TOK], bank[X_BANK][:, 0:TOK], ACT.Copy).then_inc(s_xev, 1)
                act.wait_ge(s_w_used, KC + 2 * c + 2)
                if c >= 2:
                    act.wait_ge(s_lru, c - 1)
                fn(ysil[b], bank[Y_BANK][:, 0:TOK], ACT.Gelu_apprx_tanh).then_inc(s_yev, 1)
                if c < TT:
                    act.wait_ge(s_qkms, c + 1)
                    fn(qk_ms, qk_ms, ACT.Sqrt).then_inc(s_qkroot, 1)
                if c == 0:
                    act.wait_ge(s_lam, 1)
                act.wait_ge(s_gps, c + 1)
                fn(th_r[b], bank[GATE_BANK][:, 0:TOK], ACT.Tanh, bias=half_ab[:, c:c + 1], scale=0.5
                   ).then_inc(s_gev, 1)
                fn(th_i[b], bank[GATE_BANK][:, TOK:2 * TOK], ACT.Tanh, bias=half_xb[:, c:c + 1], scale=0.5
                   ).then_inc(s_gev, 1)
                act.wait_ge(s_gev, 2 * c + 1)
                fn(decay[b], th_r[b], ACT.Exp, bias=c4[:, c:c + 1], scale=c4[:, c:c + 1]).then_inc(s_decay, 1)
                fn(drive[b], th_r[b], ACT.Tanh, bias=c4[:, c:c + 1], scale=c4[:, c:c + 1]).then_inc(s_decay, 1)
                act.wait_ge(s_mag, c + 1)
                fn(drive[b], drive[b], ACT.Sqrt, scale=-1.0).then_inc(s_sqrt, 1)
                for step, u in AFTER_CHUNK.get(c, []):
                    steps[step](u)

            act.wait_ge(s_w_used, 2 * KC)
            act.wait_ge(s_pv, UNITS)
            fn(hT[:, 0:LC, :], mixedT[:, LC:2 * LC, :], ACT.Square).then_inc(s_sqm, 1)
            act.wait_ge(s_lru, LC)
            fn(hT[:, LC:2 * LC, :], mixedT[:, 0:LC, :], ACT.Square).then_inc(s_sqm, 1)
            root(sqsum[:, :])
            root(rinv[:, :])

            with act.Fori(0, KC // WSLOTS) as i:
                for j in range(WSLOTS):
                    act.wait_ge(s_x2, i * WSLOTS + j + WSLOTS + 1)
                    act.wait_ge(s_x2add, i * WSLOTS + j + 1)
                    fn(sqb[:, j * TOK:(j + 1) * TOK].unsqueeze(1), x2T[:, bass.ds(i * WSLOTS + j, 1), :], ACT.Square
                       ).then_inc(s_x2sq, 1)
            root(rinv[:, :])
            act.wait_ge(s_adacol, 4)
            shift(SH2, KC)

            def queries(head):
                for half in range(2):
                    act.wait_ge(s_w_used, head * 2 + half + 3 * KC + 1)
                    if half == 0 and not (isinstance(head, int) and head == 0):
                        act.wait_ge(s_sps, head)
                    fn(qpT[half][:, :], bank[half][:, 0:TOK], ACT.Copy).then_inc(s_qev, 1)

            def best_exp(head):
                act.wait_ge(s_bests, head + 1)
                fn(best_e, best_e, ACT.Exp).then_inc(s_bexp, 1)

            def expert_gelu(head, t):
                act.wait_ge(s_row_used, head * (2 * TT * TOPK) + t * 2 * TOPK + TOPK + ROWS)
                fn(gel, dots, ACT.Gelu_apprx_tanh).then_inc(s_gelu, 1)

            queries(0)
            for n in range(TT * 4):
                t, quarter = divmod(n, 4)
                act.wait_ge(s_h2ps, n + 1)
                fn(h2tok[:, t, quarter * 512:(quarter + 1) * 512], bank[(3, 4, 5, 7)[n % 4]][:, :], ACT.Copy
                   ).then_inc(s_h2tok, 1)
            best_exp(0)

            def head_step(head, more):
                if more:
                    queries(head + 1)
                expert_gelu(head, 0)
                if more:
                    best_exp(head + 1)
                expert_gelu(head, 1)

            with act.Fori(0, PH - 1) as head:
                head_step(head, True)
            head_step(PH - 1, False)

            act.wait_ge(s_idx, PH)
            for n in range(4):
                act.wait_ge(s_g2ps, n + 1)
                fn(gate2[:, n * 512:(n + 1) * 512], bank[3 + n][:, :], ACT.Copy).then_inc(s_g2, 1)

        @block.vector
        def _(dve):
            v = nc.vector
            own = Chain(dve, s_dve)

            def link(ins):
                own.mark(ins)
                own.settle()

            dve.sem_inc(s_x2, WSLOTS)
            dve.sem_inc(s_row_used, ROWS)
            v.memset(ada_acc[:, 0, :], 0.0).then_inc(s_ada_used, 1)
            v.memset(ada_acc[:, 1, :], 0.0).then_inc(s_ada_used, 1)
            v.memset(ones[:, :], 1.0).then_inc(s_ones, 1)
            for b in range(2):
                own.mark(v.memset(xpad[b][:, 0:3], 0.0))
            for j in range(ROT):
                own.mark(v.memset(invf[:, j:j + 1], float(np.float32(ROPE_THETA ** (-j / ROT)))))
            dve.wait_ge(s_cols, 16)
            dve.wait_ge(s_silu, 1)
            link(v.scalar_tensor_tensor(silu_c, amp, 1.0, col("c"), ALU.add, ALU.mult))
            link(v.tensor_scalar(silu_c, silu_c, 0.5, None, ALU.mult))

            def add_piece(src, acc, k):
                return v.scalar_tensor_tensor(acc, src, silu_c[:, k] if isinstance(k, slice) else
                                              silu_c[:, bass.ds(k, 1)], acc, ALU.mult, ALU.add)

            def ada_group(g):
                with dve.Fori(0, KC // ASLOTS) as i:
                    for j in range(ASLOTS):
                        dve.wait_ge(s_ada[j], i * 16 + 16 * (g * KC // ASLOTS + 1))
                        dve.wait_ge(s_ada_used, i * ASLOTS + j + g * KC + 2)
                        add_piece(ada_ring[:, j, :], ada_acc[:, g, :], i * ASLOTS + j).then_inc(s_ada_used, 1)

            def ada_piece(n):
                g, k = divmod(n, KC)
                if k == 0:
                    dve.wait_ge(s_adaps, g - 1)
                    link(v.memset(ada_acc[:, g % 2, :], 0.0))
                dve.wait_ge(s_ada[n % ASLOTS], 16 * (n // ASLOTS + 1))
                dve.wait_ge(s_ada_used, 2 + n)
                add_piece(ada_ring[:, n % ASLOTS, :], ada_acc[:, g % 2, :], k).then_inc(s_ada_used, 1)

            def ada_column(g):
                dve.wait_ge(s_adaps, g + 1)
                v.tensor_tensor(ada_col[:, g, :], bank[ADA_BANK][:, 0:KC],
                                col("b_ada")[:, g * KC:(g + 1) * KC], ALU.add).then_inc(s_adacol, 1)
                dve.wait_ge(s_adacol, g + 1)

            means = [0]

            def mean(dst, src, n):
                means[0] += 1
                dve.wait_ge(s_stat, means[0])
                v.tensor_scalar(dst, src[:, 0:TOK], 1.0 / n, EPS, ALU.mult, ALU.add).then_inc(s_mean, 1)

            def invert(dst, n):
                dve.wait_ge(s_root, n)
                link(v.reciprocal(dst, dst))

            def modulate(gain, g, base):
                link(v.scalar_tensor_tensor(amp, ada_col[:, g, :], 1.0, col(gain), ALU.add, ALU.mult))
                with dve.Fori(0, KC) as k:
                    v.scalar_tensor_tensor(hT[:, bass.ds(k, 1), :], x2T[:, bass.ds(k, 1), :], amp[:, bass.ds(k, 1)],
                                           rinv[:, :].unsqueeze(1), ALU.mult, ALU.mult).then_inc(s_scaled, 1)

            ada_group(SH1)

            dve.wait_ge(s_pos, 16)
            link(v.tensor_copy(posf, posi))
            for t in range(TT):
                own.mark(v.tensor_scalar(angle[:, t * ROT:(t + 1) * ROT], invf, posf[:, t:t + 1], None, ALU.mult))
            own.settle()
            link(v.tensor_scalar(turns, angle, 1.0 / (2 * math.pi), None, ALU.mult))
            magic = 1.5 * 2.0 ** 23
            link(v.tensor_scalar(turns, turns, magic, None, ALU.add))
            link(v.tensor_scalar(turns, turns, magic, None, ALU.subtract))
            rest = 2 * math.pi
            for bits in (6, 18, None):
                part_ = rest if bits is None else math.floor(rest * 2.0 ** bits) / 2.0 ** bits
                rest -= part_
                link(v.scalar_tensor_tensor(angle, turns, -float(np.float32(part_)), angle, ALU.mult, ALU.add))
            v.tensor_scalar(angle, angle, 3.1415925, -3.1415925, ALU.min, ALU.max).then_inc(s_ang, 1)

            dve.wait_ge(s_lamexp, 1)
            z, zz, s, b1 = lam_t
            link(v.tensor_scalar(zz, z, 2.0, None, ALU.add))
            link(v.reciprocal(zz, zz))
            link(v.tensor_tensor(z, z, zz, ALU.mult))
            link(v.tensor_tensor(zz, z, z, ALU.mult))
            link(v.tensor_scalar(s, zz, 1.0 / 17, None, ALU.mult))
            for odd in (15, 13, 11, 9, 7, 5, 3):
                link(v.scalar_tensor_tensor(s, s, 1.0 / odd, zz, ALU.add, ALU.mult))
            link(v.scalar_tensor_tensor(s, s, 1.0, z, ALU.add, ALU.mult))
            link(v.tensor_scalar(b1, col("lam"), -1.0, 0.0, ALU.mult, ALU.max))
            link(v.scalar_tensor_tensor(s, s, 2.0, b1, ALU.mult, ALU.add))
            own.mark(v.tensor_scalar(half_ab, col("gate_a_b"), 0.5, None, ALU.mult))
            own.mark(v.tensor_scalar(half_xb, col("gate_x_b"), 0.5, None, ALU.mult))
            own.settle()
            v.tensor_scalar(c4, s, -4.0, None, ALU.mult).then_inc(s_lam, 1)

            dve.wait_ge(s_sin, 2)
            link(v.tensor_tensor(cos_t, cos_t, cos_t, ALU.mult))
            link(v.tensor_scalar(cos_t, cos_t, -2.0, 1.0, ALU.mult, ALU.add))

            mean(rinv[:, :], bank[STAT_BANK], D)
            ada_group(SC1)
            invert(rinv[:, :], 1)
            ada_column(SH1)
            ada_column(SC1)
            modulate("norm1_g", SC1, 0)

            def qk_norm(t):
                dve.wait_ge(s_qkvS, 3 * (t + 1))
                dve.wait_ge(s_rows, 16)
                q = qS[:, t, :].rearrange("p (h d) -> p h d", h=NQ)
                k = kvS[:, t, 0:P].rearrange("p (h d) -> p h d", h=NKV)
                sq = qk_square.rearrange("p (h d) -> p h d", h=NQK)
                own.mark(v.tensor_tensor(sq[:, 0:NQ, :], q, q, ALU.mult))
                own.mark(v.tensor_tensor(sq[:, NQ:NQK, :], k, k, ALU.mult))
                own.settle()
                link(v.tensor_reduce(qk_ms, sq, AX, ALU.add))
                v.tensor_scalar(qk_ms, qk_ms, 1.0 / HD, EPS, ALU.mult, ALU.add).then_inc(s_qkms, 1)
                dve.wait_ge(s_qkroot, t + 1)
                link(v.reciprocal(qk_ms, qk_ms))
                sides = ((q, NQ, qk_ms[:, 0:NQ], q_gain), (k, NKV, qk_ms[:, NQ:NQK], k_gain))
                for x, n, r, _ in sides:
                    own.mark(v.tensor_tensor(x, x, spread(r, HD, 2), ALU.mult))
                own.settle()
                for x, n, _, gain in sides:
                    own.mark(v.tensor_tensor(x, x, spread(gain, n, 1), ALU.mult))
                own.settle()
                sin, cos = sin_t[:, t * ROT:(t + 1) * ROT], cos_t[:, t * ROT:(t + 1) * ROT]
                places = []
                for x, n, base in ((q, NQ, 0), (k, NKV, 4 * NQ * ROT)):
                    tmp = qk_square[:, base:base + 4 * n * ROT].rearrange("p (a h d) -> p a h d", a=4, h=n)
                    places.append((x, tmp))
                    for a, (half, w) in enumerate(((0, cos), (1, sin), (1, cos), (0, sin))):
                        own.mark(v.tensor_tensor(tmp[:, a], x[:, :, half * ROT:(half + 1) * ROT],
                                                 spread(w, n, 1), ALU.mult))
                own.settle()
                for x, tmp in places:
                    own.mark(v.tensor_tensor(x[:, :, 0:ROT], tmp[:, 0], tmp[:, 1], ALU.subtract))
                    own.mark(v.tensor_tensor(x[:, :, ROT:2 * ROT], tmp[:, 2], tmp[:, 3], ALU.add))
                own.settle()
                for u in range(2):
                    last = v.tensor_copy(kdup[:, t, :, u, :], k)
                    if u == 0:
                        own.mark(last)
                own.settle()
                last.then_inc(s_qk, 1)

            def qk_transpose(_):
                pass

            def scores(u):
                t, heads, keys_n = unit_heads(u)
                n = len(heads)
                pr = probs[u % 2][:, 0:n * (keys_n + 1)].rearrange("p (h k) -> p h k", h=n)
                if u >= 2:
                    dve.wait_ge(s_PTps, 2 * (u - 1))
                for o in range(2):
                    own.mark(v.tensor_copy(pr[:, o * n // 2:(o + 1) * n // 2, keys_n:keys_n + 1],
                                           sink[:, heads[0] + o:heads[0] + n:2].unsqueeze(2)))
                dve.wait_ge(s_scps, u + 1)
                for o, b in enumerate((EVEN_BANK, ODD_BANK)):
                    v.scalar_tensor_tensor(pr[:, o * n // 2:(o + 1) * n // 2, 0:keys_n],
                                           bank[b][:, :].rearrange("p (h k) -> p h k", h=n // 2), HD ** -0.5,
                                           spread(mask[t], n // 2, 1), ALU.mult, ALU.add).then_inc(s_scS, 1)
                own.settle()
                dve.wait_ge(s_scS, 2 * u + 2)
                link(v.tensor_reduce(mx[:, 0:n], pr, AX, ALU.max))
                v.tensor_tensor(pr, pr, spread(mx[:, 0:n], keys_n + 1, 2), ALU.subtract).then_inc(s_shift, 1)
                dve.wait_ge(s_exp, u + 1)
                link(v.tensor_reduce(den[:, 0:n], pr, AX, ALU.add))
                link(v.reciprocal(den[:, 0:n], den[:, 0:n]))
                v.tensor_tensor(pr[:, :, 0:keys_n], pr[:, :, 0:keys_n], spread(den[:, 0:n], keys_n, 2),
                                ALU.mult).then_inc(s_prob, 1)

            steps = {"qk_transpose": qk_transpose, "scores": scores, "values": qk_transpose}
            done = 2 * KC
            for c in range(LC):
                b = c % 2
                dve.wait_ge(s_xev, c + 1)
                if c >= 2:
                    dve.wait_ge(s_gps, c - 1)
                taps = [colv[:, COLS["conv_w"][0] + k * LC + c:COLS["conv_w"][0] + k * LC + c + 1] for k in range(4)]
                link(v.tensor_scalar(xconv[b], xpad[b][:, 0:TOK], taps[0], col("conv_b", c), ALU.mult, ALU.add))
                for k in range(1, 4):
                    ins = v.scalar_tensor_tensor(xconv[b], xpad[b][:, k:k + TOK], taps[k], xconv[b],
                                                 ALU.mult, ALU.add)
                    if k < 3:
                        link(ins)
                ins.then_inc(s_conv, 1)
                if c < TT:
                    qk_norm(c)
                ada_piece(done)
                dve.wait_ge(s_decay, 2 * c + 2)
                link(v.tensor_tensor(bscan, decay[b], decay[b], ALU.mult))
                v.scalar_tensor_tensor(drive[b], bscan, 1.0, drive[b], ALU.add, ALU.mult).then_inc(s_mag, 1)
                ada_piece(done + 1)
                dve.wait_ge(s_mag, c + 1)
                dve.wait_ge(s_conv, c + 1)
                link(v.scalar_tensor_tensor(bscan, th_i[b], 1.0, xconv[b], ALU.add, ALU.mult))
                dve.wait_ge(s_sqrt, c + 1)
                link(v.scalar_tensor_tensor(bscan, bscan, 0.5, drive[b], ALU.mult, ALU.mult))
                link(v.tensor_tensor_scan(mixedT[:, c, :], decay[b], bscan, 0.0, ALU.mult, ALU.add))
                dve.wait_ge(s_yev, c + 1)
                v.tensor_tensor(mixedT[:, c, :], mixedT[:, c, :], ysil[b], ALU.mult).then_inc(s_lru, 1)
                ada_piece(done + 2)
                done += 3
                for step, u in AFTER_CHUNK.get(c, []):
                    steps[step](u)

            mean(sqsum[:, :], bank[STAT_BANK], LRU)
            mean(rinv[:, :], bank[PT_BANK], LRU)
            ada_column(G1)
            invert(sqsum[:, :], 2)
            invert(rinv[:, :], 3)
            for k in range(KC):
                v.scalar_tensor_tensor(mixedT[:, k, :], mixedT[:, k, :], col("out_g", k),
                                       (rinv if k < LC else sqsum)[:, :], ALU.mult, ALU.mult).then_inc(s_mix, 1)
            for c in range(KC):
                dve.wait_ge(s_w_used, 2 * KC + c + 1)
                v.scalar_tensor_tensor(x2T[:, c, :], bank[c % WSLOTS][:, 0:TOK], ada_col[:, G1, c:c + 1],
                                       x2T[:, c, :], ALU.mult, ALU.add).then_inc(s_x2, 1)
                for _ in range(1 + c % 2):
                    ada_piece(done)
                    done += 1
            ada_column(SH2)
            ada_column(SC2)
            mean(rinv[:, :], bank[STAT_BANK], D)
            invert(rinv[:, :], 4)
            dve.wait_ge(s_x2, WSLOTS + KC)
            modulate("norm2_g", SC2, KC)
            link(v.memset(ada_acc[:, 1, :], 0.0))

            def top16(values_, src, at_):
                for j in range(len(src)):
                    own.mark(v.max(values_[j][:, 0:8], src[j]))
                own.settle()
                for j in range(len(src)):
                    own.mark(v.max_index(at_[j][:, 0:8], values_[j][:, 0:8], src[j]))
                own.settle()
                for j in range(len(src)):
                    own.mark(v.match_replace(src[j], values_[j][:, 0:8], src[j], GONE))
                own.settle()
                for j in range(len(src)):
                    own.mark(v.max(values_[j][:, 8:16], src[j]))
                own.settle()
                for j in range(len(src)):
                    own.mark(v.max_index(at_[j][:, 8:16], values_[j][:, 8:16], src[j]))
                own.settle()

            def select(head, parity):
                dve.wait_ge(s_sps, head + 1)
                link(v.tensor_copy(sc_s, bank[2][:, :]))
                sets = [(a, t) for a in range(2) for t in range(TT)]
                top16([top_v[:, a, t, :] for a, t in sets],
                      [sc_s[:, (a * TT + t) * NKEY:(a * TT + t + 1) * NKEY] for a, t in sets],
                      [top_i[:, a, t, :] for a, t in sets])
                own.mark(v.tensor_scalar(top_f[:, 0], top_i[:, 0], float(NKEY), None, ALU.mult))
                own.mark(v.tensor_copy(top_f[:, 1], top_i[:, 1]))
                own.settle()
                off = 0
                for i0, r, n in RECTS:
                    for dst, src in ((cand_s, top_v), (cand_i, top_f)):
                        own.mark(v.tensor_tensor(
                            dst[:, :, off:off + r * n].rearrange("p t (r n) -> p t r n", r=r),
                            spread(src[:, 0, :, i0:i0 + r], n, 3), spread(src[:, 1, :, 0:n], r, 2), ALU.add))
                    off += r * n
                own.settle()
                top16([best_v[:, t, :] for t in range(TT)], [cand_s[:, t, :] for t in range(TT)],
                      [best_p[:, t, :] for t in range(TT)])
                v.tensor_tensor(best_e, best_v, best_v[:, :, 0:1].broadcast_to([P, TT, TOPK]), ALU.subtract
                                ).then_inc(s_bests, 1)
                link(v.tensor_copy(best_f, best_p))
                for t in range(TT):
                    link(v.tensor_tensor(hot, spread(best_f[:, t, :], NCAND, 2), spread(iota_c, TOPK, 1),
                                         ALU.is_equal))
                    link(v.tensor_tensor(hot, hot, spread(cand_i[:, t, :], TOPK, 1), ALU.mult))
                    link(v.tensor_reduce(best_v[:, t, :], hot, AX, ALU.add))
                v.tensor_copy(idx[parity], best_v.rearrange("p t k -> p (t k)")).then_inc(s_idx, 1)
                dve.wait_ge(s_bexp, head + 1)
                link(v.tensor_reduce(tksum, best_e, AX, ALU.add))
                link(v.reciprocal(tksum, tksum))
                link(v.tensor_tensor(gsm[parity].rearrange("p (t k) -> p t k", t=TT), best_e,
                                     spread(tksum, TOPK, 2), ALU.mult))

            def experts(i, parity, t):
                base = (parity * TT + t) * 2 * TOPK
                for k in range(TOPK):
                    local = base + k
                    dve.wait_ge(s_row[local % ROWS], i * (16 * PAIR_ROWS // ROWS) + 16 * (local // ROWS + 1))
                    v.tensor_tensor_reduce(ring_row(local % ROWS), ring_row(local % ROWS), h2tok[:, t, :], 1.0, 0.0,
                                           ALU.mult, ALU.add, dots[:, k:k + 1]).then_inc(s_row_used, 1)
                if t == 0:
                    for j in range(LATE_ASLOTS):
                        n = parity * LATE_ASLOTS + j
                        dve.wait_ge(s_ada_late[j], i * 32 + 16 * (parity + 1))
                        dve.wait_ge(s_ada_used, i * 4 + n + 5 * KC + 2)
                        add_piece(ada_ring[:, j, :], ada_acc[:, 1, :], i * 4 + n).then_inc(s_ada_used, 1)
                dve.wait_ge(s_gelu, i * 2 * TT + parity * TT + t + 1)
                link(v.tensor_tensor(wgt, gel, gsm[parity][:, t * TOPK:(t + 1) * TOPK], ALU.mult))
                for k in range(TOPK):
                    local = base + TOPK + k
                    dve.wait_ge(s_row[local % ROWS], i * (16 * PAIR_ROWS // ROWS) + 16 * (local // ROWS + 1))
                    dve.wait_ge(s_row_used, i * PAIR_ROWS + local + ROWS)
                    v.scalar_tensor_tensor(peer[:, t, :], ring_row(local % ROWS), wgt[:, k:k + 1], peer[:, t, :],
                                           ALU.mult, ALU.add).then_inc(s_row_used, 1)

            def head_pair(i, more):
                experts(i, 0, 0)
                select(i * 2 + 1, 1)
                experts(i, 0, 1)
                experts(i, 1, 0)
                if more:
                    select(i * 2 + 2, 0)
                experts(i, 1, 1)

            dve.wait_ge(s_const, 10)
            select(0, 0)
            dve.wait_ge(s_h2tok, TT * 4)
            own.restart()
            with dve.Fori(0, PH // 2 - 1) as i:
                head_pair(i, True)
                own.restart()
            head_pair(PH // 2 - 1, False)

            dve.wait_ge(s_g2, 4)
            dve.wait_ge(s_row_used, ROWS + PH * TT * 2 * TOPK)
            for t in range(TT):
                link(v.tensor_tensor(peer[:, t, :], peer[:, t, :], gate2, ALU.mult))
                for n in range(4):
                    dve.wait_ge(s_x2ps, 4 * t + n + 1)
                    part_ = peer[:, t, n * 512:(n + 1) * 512]
                    v.tensor_tensor(part_, part_, bank[((0, 1, 2, 7), (3, 4, 5, 6))[t][n]][:, :], ALU.add
                                    ).then_inc(s_fin, 1)


def kernel(**inputs):
    import concourse.bacc as bacc
    from concourse.bass_utils import run_bass_kernel_spmd

    a = {n: np.asarray(x) for n, x in inputs.items()}

    def columns(v):
        return v.reshape(-1, P).T

    w_in, depth = a["w_in"][0], 0
    halves = w_in[:, 0:2 * LRU].reshape(KC, P, 2, LC, P)

    def chunks(w):
        return w.reshape(KC, P, -1, P).transpose(2, 1, 0, 3).reshape(-1, P, D)

    arrays = {
        "xT": a["x"][0].T.reshape(KC, P, TOK).transpose(1, 0, 2).reshape(P, KC * TOK),
        "cols": np.concatenate([columns(a[n][0]) for n in ("c", "b_ada", "norm1_g", "norm2_g")]
                               + [columns(a["out_norm_lru_g"][0]), columns(a["out_norm_attn_g"][0])]
                               + [columns(a[n][0]) for n in ("conv_w", "conv_b", "lru_gate_a_b", "lru_gate_x_b",
                                                             "lru_lambda")], axis=1),
        "rowv": np.broadcast_to(np.concatenate([a["q_norm_g"][0], a["k_norm_g"][0], a["attn_sinks"][0]]), (P, NROWV)),
        "pos": a["positions"][0].reshape(TT, P).T,
        "w_ada": a["w_ada"][0].reshape(KC, P, ADA_GROUPS, D).transpose(2, 0, 1, 3).reshape(ADA_GROUPS * KC, P, D),
        "b_gate2": a["b_ada"][:, 5 * D:],
        "w_qkv": w_in[:, 2 * LRU:].reshape(KC, P, QKV),
        "w_chunks": np.concatenate([halves.transpose(3, 2, 1, 0, 4).reshape(KC, P, D), chunks(a["w_out"][0]),
                                    chunks(a["peer_w_q"][0])]),
        "gates": np.stack([a["lru_gate_a_w"][0], a["lru_gate_x_w"][0]]).transpose(2, 0, 1, 3).reshape(P, 2 * LC * P),
        "keys": a["peer_sub_keys"][0].transpose(3, 0, 1, 2).reshape(P, 2 * PH * NKEY),
        "peer_u": a["peer_u"][0],
        "peer_v": a["peer_v"][0],
    }
    nc = bacc.Bacc("TRN2", target_bir_lowering=False, num_devices=1)
    sent, args = {}, []
    for name, x in arrays.items():
        x = np.ascontiguousarray(x)
        sent[f"in_{name}"] = x
        args.append(nc.dram_tensor(f"in_{name}", x.shape, mybir.dt.from_np(x.dtype), kind="ExternalInput").ap())
    result = nc.dram_tensor("result", (TOK, D), F32, kind="ExternalOutput").ap()
    build(nc, *args, result)
    r = run_bass_kernel_spmd(nc, [sent], core_ids=[0])
    return r.results[0]["result"].reshape(1, TOK, D)
```

```python
import itertools
import math
from contextlib import ExitStack

import numpy as np

import concourse.bass as bass
from concourse import mybir

P = 128
D = 2048
TOK = 256
KC = D // P
TT = TOK // P
LRU = 1024
LC = LRU // P
HD = 64
NQ, NKV = 16, 2
NQK = NQ + NKV
QKV = (NQ + 2 * NKV) * HD
ROT = 8
ROPE_THETA = 500000.0
PH = 8
NKEY = 128
TOPK = 16
EPS = 1e-6
ADA_GROUPS = 6
SH1, SC1, G1, SH2, SC2, G2 = range(ADA_GROUPS)
NEG = -1e30
GONE = -3e38

RECTS = [(0, 1, 16), (1, 1, 8), (2, 2, 5), (4, 4, 3), (8, 8, 1)]
NCAND = sum(r * c for _, r, c in RECTS)

WSLOTS = 4
ASLOTS = 4
ROWS = 8
PAIR_ROWS = 2 * TT * 2 * TOPK

COLS = {}
_at = 0
for _name, _n in (("c", KC), ("b_ada", ADA_GROUPS * KC), ("norm1_g", KC), ("norm2_g", KC), ("out_g", KC),
                  ("conv_w", 4 * LC), ("conv_b", LC), ("gate_a_b", LC), ("gate_x_b", LC), ("lam", LC)):
    COLS[_name] = (_at, _at + _n)
    _at += _n
NCOLS = _at
NROWV = 2 * HD + NQ

ALU = mybir.AluOpType
ACT = mybir.ActivationFunctionType
AX = mybir.AxisListType.X
F32 = mybir.dt.float32
I32 = mybir.dt.int32
U32 = mybir.dt.uint32


class Chain:

    def __init__(self, engine, sem):
        self.engine, self.sem, self.count = engine, sem, 0

    def mark(self, ins):
        ins.then_inc(self.sem, 1)
        self.count += 1

    def settle(self):
        if self.count:
            self.engine.wait_ge(self.sem, self.count)

    def restart(self):
        self.settle()
        self.engine.sem_clear(self.sem)
        self.count = 0


def pairs_before(u):
    return sum(len(unit_heads(w)[1]) // 2 for w in range(u))


def unit_heads(u):
    t, first, n = (0, 8 * u, 8) if u < 2 else (1, 4 * (u - 2), 4)
    heads = list(range(first, first + n, 2)) + list(range(first + 1, first + n, 2))
    return t, heads, P * (t + 1)


MIX_ORDER = list(range(LC, 2 * LC)) + list(range(LC))
UNITS = 6
FIRST_UNIT_CHUNK = 2
MID_ADA = 3 * KC


def build(nc, xT, cols, rowv, pos, w_ada, b_gate2, w_qkv, w_chunks, gates, keys, peer_u, peer_v, out):
    with ExitStack() as ctx:
        def sb(name, shape, dt=F32):
            return ctx.enter_context(nc.sbuf_tensor(name, shape, dt))

        def sem(name):
            return ctx.enter_context(nc.semaphore(name))

        x2T = sb("x2T", [P, KC, TOK])
        hT = sb("hT", [P, KC, TOK])
        mixedT = sb("mixedT", [P, KC, TOK])
        h2tok = mixedT[:, :, :].rearrange("p a b -> p (a b)").rearrange("p (t d) -> p t d", t=TT)
        peer = sb("peer", [P, TT, D])
        w_ring = sb("w_ring", [P, WSLOTS, D])
        ada_ring = sb("ada_ring", [P, ASLOTS, D])
        ada_acc = sb("ada_acc", [P, 2, D])
        keysT = sb("keysT", [P, 2 * PH, NKEY])
        mixer = sb("mixer", [P, 6 * D])
        colv = sb("colv", [P, NCOLS])
        rows = sb("rows", [P, NROWV])
        ident = sb("ident", [P, P])
        ones = sb("ones", [P, P])
        small = sb("small", [P, 528])

        peer_flat = peer[:, :, :].rearrange("p t d -> p (t d)")
        gate_w = peer_flat[:, 0:2048].rearrange("p (g c n) -> p g c n", g=2, c=LC)
        qS = peer_flat[:, 2048:4096].rearrange("p (t q) -> p t q", t=TT)

        cut = [0]

        def part(n):
            cut[0] += n
            assert cut[0] <= 6 * D
            return mixer[:, cut[0] - n:cut[0]]

        kvS = part(512).rearrange("p (t n) -> p t n", t=TT)
        kdup = part(512).rearrange("p (t k u d) -> p t k u d", t=TT, k=NKV, u=2)
        qTr = part(2048).rearrange("p (t h n) -> p t h n", t=TT, h=8)
        kTr = part(512).rearrange("p (k n) -> p k n", k=NKV)
        probs = [part(8 * 129) for _ in range(2)]
        probsT = [part(1024) for _ in range(2)]
        qk_square = mixer[:, cut[0] - 2048 - 2 * 8 * 129:cut[0] - 2048 - 2 * 8 * 129 + NQK * HD]
        xpad = [part(260) for _ in range(2)]
        xconv = [part(TOK) for _ in range(2)]
        th_r = [part(TOK) for _ in range(2)]
        th_i = [part(TOK) for _ in range(2)]
        decay = [part(TOK) for _ in range(2)]
        drive = [part(TOK) for _ in range(2)]
        ysil = [part(TOK) for _ in range(2)]
        bscan = part(TOK)

        def ring_row(slot):
            if slot < 6:
                return mixer[:, slot * D:(slot + 1) * D]
            return ada_ring[:, ASLOTS - 2 + slot - 6, :]

        mask = [part(P), part(2 * P)]
        attn_sq = part(P)
        lru_sq = sb("lru_sq", [P, TOK])
        rinv = sb("rinv", [P, TOK])
        sqsum = sb("sqsum", [P, TOK])
        lru_sum, attn_sum = rinv, sqsum
        qpT = [sqsum, rinv]
        sqb = probs[0]

        at = [0]

        def little(n, dt=F32):
            at[0] += n
            assert at[0] <= 528
            v = small[:, at[0] - n:at[0]]
            return v if dt == F32 else v.bitcast(dt)

        silu_c = little(KC)
        ada_col = little(5 * KC).rearrange("p (g k) -> p g k", g=5)
        amp = little(KC)
        c4 = little(LC)
        half_ab = little(LC)
        half_xb = little(LC)
        angle = little(TT * ROT)
        turns = little(TT * ROT)
        sin_t = little(TT * ROT)
        cos_t = little(TT * ROT)
        invf = little(ROT)
        posf = little(TT)
        posi = little(TT, I32)
        qk_ms = little(NQK)
        mx = little(8)
        den = little(8)
        lam_t = [little(LC) for _ in range(4)]
        iota_c = little(NCAND)
        idx = [little(TT * TOPK, U32) for _ in range(2)]
        gsm = [little(TT * TOPK) for _ in range(2)]
        dots = little(TOPK)
        gel = little(TOPK)
        wgt = little(TOPK)
        tick = little(ROWS + 1)
        tksum = little(TT)

        tk = [0]

        def topk_part(n, dt=F32):
            tk[0] += n
            assert tk[0] <= D
            v = ada_acc[:, 0, tk[0] - n:tk[0]]
            return v if dt == F32 else v.bitcast(dt)

        sc_s = topk_part(2 * TT * NKEY)
        top_v = topk_part(2 * TT * TOPK).rearrange("p (a t k) -> p a t k", a=2, t=TT)
        top_i = topk_part(2 * TT * TOPK, U32).rearrange("p (a t k) -> p a t k", a=2, t=TT)
        top_f = topk_part(2 * TT * TOPK).rearrange("p (a t k) -> p a t k", a=2, t=TT)
        cand_s = topk_part(TT * NCAND).rearrange("p (t c) -> p t c", t=TT)
        cand_i = topk_part(TT * NCAND).rearrange("p (t c) -> p t c", t=TT)
        best_v = topk_part(TT * TOPK).rearrange("p (t k) -> p t k", t=TT)
        best_p = topk_part(TT * TOPK, U32).rearrange("p (t k) -> p t k", t=TT)
        best_e = topk_part(TT * TOPK).rearrange("p (t k) -> p t k", t=TT)
        best_f = topk_part(TT * TOPK).rearrange("p (t k) -> p t k", t=TT)
        hot = topk_part(TOPK * NCAND).rearrange("p (k c) -> p k c", k=TOPK)
        gate2 = ada_acc[:, 1, :]
        brow = ada_ring[0:1, 0, :]

        bank = [ctx.enter_context(nc.psum_tensor(f"bank{i}", [P, 512], F32)) for i in range(8)]
        X_BANK, Y_BANK, GATE_BANK, EVEN_BANK, ODD_BANK, PT_BANK, ADA_BANK, STAT_BANK = range(8)

        s_cols, s_xin, s_rows, s_pos, s_gatew, s_keys, s_brow = map(
            sem, ("s_cols", "s_xin", "s_rows", "s_pos", "s_gatew", "s_keys", "s_brow"))
        s_w = [sem(f"s_w{i}") for i in range(WSLOTS)]
        s_w_used = sem("s_w_used")
        s_ada = [sem(f"s_ada{i}") for i in range(ASLOTS)]
        s_ada_used = sem("s_ada_used")
        s_const = sem("s_const")
        s_ones = sem("s_ones")
        s_dve, s_act = sem("s_dve"), sem("s_act")
        s_silu, s_cvec = sem("s_silu"), sem("s_cvec")
        s_sq1 = sem("s_sq1")
        s_stat, s_mean, s_root = sem("s_stat"), sem("s_mean"), sem("s_root")
        s_adaps, s_adacol = sem("s_adaps"), sem("s_adacol")
        s_scaled, s_h = sem("s_scaled"), sem("s_h")
        s_qkvps, s_qkvS = sem("s_qkvps"), sem("s_qkvS")
        s_ang, s_sin = sem("s_ang"), sem("s_sin")
        s_lamabs, s_lamexp, s_lam = sem("s_lamabs"), sem("s_lamexp"), sem("s_lam")
        s_qkms, s_qkroot, s_qk = sem("s_qkms"), sem("s_qkroot"), sem("s_qk")
        s_qkTps, s_qkT = sem("s_qkTps"), sem("s_qkT")
        s_xps, s_yps, s_gps = sem("s_xps"), sem("s_yps"), sem("s_gps")
        s_xev, s_conv, s_yev, s_gev = sem("s_xev"), sem("s_conv"), sem("s_yev"), sem("s_gev")
        s_decay, s_mag, s_sqrt, s_lru = sem("s_decay"), sem("s_mag"), sem("s_sqrt"), sem("s_lru")
        s_scps, s_scS, s_shift, s_exp, s_prob = (
            sem("s_scps"), sem("s_scS"), sem("s_shift"), sem("s_exp"), sem("s_prob"))
        s_PTps, s_PT, s_pvps, s_pv = sem("s_PTps"), sem("s_PT"), sem("s_pvps"), sem("s_pv")
        s_mix = sem("s_mix")
        s_lrusq, s_lrusum, s_attnsq, s_attnsum = sem("s_lrusq"), sem("s_lrusum"), sem("s_attnsq"), sem("s_attnsum")
        s_ops, s_x2, s_x2sq, s_x2add = sem("s_ops"), sem("s_x2"), sem("s_x2sq"), sem("s_x2add")
        s_qps, s_qev, s_sps, s_sS = sem("s_qps"), sem("s_qev"), sem("s_sps"), sem("s_sS")
        s_h2ps, s_h2tok = sem("s_h2ps"), sem("s_h2tok")
        s_bests, s_bexp, s_idx = sem("s_bests"), sem("s_bexp"), sem("s_idx")
        s_row = [sem(f"s_row{i}") for i in range(ROWS)]
        s_row_used = sem("s_row_used")
        s_hold = sem("s_hold")
        s_gelu = sem("s_gelu")
        s_g2ps, s_g2 = sem("s_g2ps"), sem("s_g2")
        s_x2ps, s_fin, s_out = sem("s_x2ps"), sem("s_fin"), sem("s_out")

        def col(name, k=None):
            a, b = COLS[name]
            return colv[:, a:b] if k is None else colv[:, a + k:a + k + 1]

        q_gain, k_gain, sink = rows[:, 0:HD], rows[:, HD:2 * HD], rows[:, 2 * HD:2 * HD + NQ]

        def spread(ap, n, axis):
            wide = ap.unsqueeze(axis)
            shape = list(wide.shape)
            shape[axis] = n
            return wide.broadcast_to(shape)

        def piece(stack, n):
            return stack[bass.ds(n, 1)].rearrange("a p n -> (a p) n")

        block = ctx.enter_context(nc.Block())

        @block.sync
        def _(sp):
            sp.dma_start(colv[:, :], cols).then_inc(s_cols, 16)
            for j in range(ASLOTS):
                sp.dma_start(ada_ring[:, j, :], w_ada[j]).then_inc(s_ada[j], 16)
            sp.dma_start(x2T[:, :, :], xT.rearrange("p (k t) -> p k t", k=KC)).then_inc(s_xin, 16)
            sp.dma_start(rows[:, :], rowv).then_inc(s_rows, 16)
            sp.dma_start(posi, pos).then_inc(s_pos, 16)
            with sp.Fori(1, 2 * KC // ASLOTS) as i:
                for j in range(ASLOTS):
                    sp.wait_ge(s_ada_used, i * ASLOTS + j - ASLOTS + 3)
                    sp.dma_start(ada_ring[:, j, :], piece(w_ada, i * ASLOTS + j)).then_inc(s_ada[j], 16)
            for j in range(WSLOTS):
                sp.dma_start(w_ring[:, j, 0:QKV], w_qkv[j]).then_inc(s_w[j], 16)
            with sp.Fori(0, KC // WSLOTS - 1) as i:
                for j in range(WSLOTS):
                    sp.wait_ge(s_ada_used, 2 * KC + i * ASLOTS + j - ASLOTS + 3)
                    sp.dma_start(ada_ring[:, j, :], piece(w_ada, 2 * KC + i * ASLOTS + j)).then_inc(s_ada[j], 16)
                    sp.wait_ge(s_w_used, i * WSLOTS + j + 1)
                    sp.dma_start(w_ring[:, j, 0:QKV], piece(w_qkv, (i + 1) * WSLOTS + j)).then_inc(s_w[j], 16)
            for j in range(ASLOTS):
                sp.wait_ge(s_ada_used, 3 * KC + j - 2 * ASLOTS + 3)
                sp.dma_start(ada_ring[:, j, :], w_ada[3 * KC - ASLOTS + j]).then_inc(s_ada[j], 16)
            sp.dma_start(gate_w, gates.rearrange("p (g c n) -> p g c n", g=2, c=LC)).then_inc(s_gatew, 16)
            with sp.Fori(0, 4) as i:
                for j in range(12):
                    if j % 3 != 2:
                        w = j // 3 * 2 + j % 3
                        sp.wait_ge(s_w_used, KC + i * 8 + w - WSLOTS + 1)
                        sp.dma_start(w_ring[:, w % WSLOTS, :], piece(w_chunks, i * 8 + w)
                                     ).then_inc(s_w[w % WSLOTS], 16)
                    sp.wait_ge(s_ada_used, 3 * KC + i * 12 + j - ASLOTS + 3)
                    sp.dma_start(ada_ring[:, j % ASLOTS, :], piece(w_ada, 3 * KC + i * 12 + j)
                                 ).then_inc(s_ada[j % ASLOTS], 16)
            for j in range(WSLOTS):
                sp.wait_ge(s_w_used, 3 * KC + j - WSLOTS + 1)
                sp.dma_start(w_ring[:, j, :], w_chunks[2 * KC + j]).then_inc(s_w[j], 16)
                if j == 1:
                    sp.dma_start(keysT[:, :, :], keys.rearrange("p (c n) -> p c n", c=2 * PH)).then_inc(s_keys, 16)
            sp.wait_ge(s_ada_used, ADA_GROUPS * KC + 2)
            sp.dma_start(brow, b_gate2).then_inc(s_brow, 16)
            with sp.Fori(1, 4) as i:
                for j in range(WSLOTS):
                    sp.wait_ge(s_w_used, 3 * KC + i * WSLOTS + j - WSLOTS + 1)
                    sp.dma_start(w_ring[:, j, :], piece(w_chunks, 2 * KC + i * WSLOTS + j)).then_inc(s_w[j], 16)
            for t in range(TT):
                for n in range(4):
                    sp.wait_ge(s_fin, 4 * t + n + 1)
                    sp.dma_start(out[t * P:(t + 1) * P, n * 512:(n + 1) * 512], peer[:, t, n * 512:(n + 1) * 512]
                                 ).then_inc(s_out, 16)
            sp.wait_ge(s_out, 16 * TT * 4)

        @block.gpsimd
        def _(pool):
            g = nc.gpsimd
            g.memset(ident[:, :], 0.0).then_inc(s_const, 1)
            g.memset(mask[0], 0.0).then_inc(s_const, 1)
            g.memset(mask[1], 0.0).then_inc(s_const, 1)
            g.memset(tick[:, ROWS:ROWS + 1], 0.0).then_inc(s_const, 1)
            g.memset(tick[:, 0:ROWS], 0.0).then_inc(s_hold, ROWS)
            g.iota(iota_c, pattern=[[1, NCAND]], base=0, channel_multiplier=0,
                   allow_small_or_imprecise_dtypes=True).then_inc(s_const, 1)
            pool.wait_ge(s_const, 5)
            g.affine_select(out=ident[:, :], in_=ident[:, :], compare_op=ALU.not_equal, fill=1.0, base=0,
                            pattern=[[-1, P]], channel_multiplier=1).then_inc(s_const, 1)
            g.affine_select(out=mask[0], in_=mask[0], compare_op=ALU.is_ge, fill=NEG, base=0,
                            pattern=[[-1, P]], channel_multiplier=1).then_inc(s_const, 1)
            g.affine_select(out=mask[1][:, 0:P], in_=mask[1][:, 0:P], compare_op=ALU.is_ge, fill=NEG, base=-1,
                            pattern=[[1, P]], channel_multiplier=-1).then_inc(s_const, 1)
            g.affine_select(out=mask[1][:, P:2 * P], in_=mask[1][:, P:2 * P], compare_op=ALU.is_ge, fill=NEG,
                            base=0, pattern=[[-1, P]], channel_multiplier=1).then_inc(s_const, 1)
            pool.wait_ge(s_scaled, KC)
            g.memset(lru_sum[:, :], 0.0).then_inc(s_lrusum, 1)
            g.memset(attn_sum[:, :], 0.0).then_inc(s_attnsum, TT)
            for c in range(LC):
                pool.wait_ge(s_lru, c + 1)
                pool.wait_ge(s_lrusum, c + 1)
                g.tensor_tensor(lru_sq[:, :], mixedT[:, c, :], mixedT[:, c, :], ALU.mult).then_inc(s_lrusq, 1)
                pool.wait_ge(s_lrusq, c + 1)
                g.tensor_tensor(lru_sum[:, :], lru_sum[:, :], lru_sq[:, :], ALU.add).then_inc(s_lrusum, 1)
                u = c - FIRST_UNIT_CHUNK
                if u >= 0:
                    t, heads, _ = unit_heads(u)
                    pool.wait_ge(s_pv, u + 1)
                    for pair in range(heads[0] // 2, heads[0] // 2 + len(heads) // 2):
                        o = mixedT[:, LC + pair, t * P:(t + 1) * P]
                        done_ = pairs_before(u) + pair - heads[0] // 2
                        pool.wait_ge(s_attnsum, TT + done_)
                        g.tensor_tensor(attn_sq[:, :], o, o, ALU.mult).then_inc(s_attnsq, 1)
                        pool.wait_ge(s_attnsq, done_ + 1)
                        sum_ = attn_sum[:, t * P:(t + 1) * P]
                        g.tensor_tensor(sum_, sum_, attn_sq[:, :], ALU.add).then_inc(s_attnsum, 1)
            pool.wait_ge(s_mix, KC)
            g.memset(sqsum[:, :], 0.0).then_inc(s_x2add, WSLOTS)
            g.memset(peer[:, :, :], 0.0).then_inc(s_const, 1)
            with pool.Fori(0, KC // WSLOTS) as i:
                for j in range(WSLOTS):
                    pool.wait_ge(s_x2sq, i * WSLOTS + j + 1)
                    pool.wait_ge(s_x2add, i * WSLOTS + j + WSLOTS)
                    g.tensor_tensor(sqsum[:, :], sqsum[:, :], sqb[:, j * TOK:(j + 1) * TOK],
                                    ALU.add).then_inc(s_x2add, 1)
            with pool.Fori(0, PH // 2) as i:
                for local in range(PAIR_ROWS):
                    group, k = divmod(local, 2 * TOPK)
                    parity, t = divmod(group, TT)
                    table = peer_u if k < TOPK else peer_v
                    slot, c = local % ROWS, t * TOPK + k % TOPK
                    if local % (2 * TT * TOPK) == 0:
                        pool.wait_ge(s_idx, i * 2 + parity + 1)
                    pool.wait_ge(s_row_used, i * PAIR_ROWS + local + 1)
                    pool.wait_ge(s_hold, i * PAIR_ROWS + local + 1)
                    g.tensor_tensor(tick[:, slot:slot + 1], tick[:, ROWS:ROWS + 1], tick[:, ROWS:ROWS + 1],
                                    ALU.add).then_inc(s_hold, 1)
                    g.indirect_dma_start(ring_row(slot), None, table,
                                         bass.IndirectOffsetOnAxis(ap=idx[parity][:, c:c + 1], axis=0)
                                         ).then_inc(s_row[slot], 16)

        @block.tensor
        def _(pe):
            mm = nc.tensor.matmul

            def column_sums(g):
                pe.wait_ge(s_ada_used, 2 + (g + 1) * KC)
                if g:
                    pe.wait_ge(s_adacol, g)
                for k in range(KC):
                    last = mm(bank[ADA_BANK][:, k:k + 1], ada_acc[:, g % 2, k * P:(k + 1) * P], ones[:, 0:1],
                              start=True, stop=True)
                last.then_inc(s_adaps, 1)

            def token_sums(dst, parts):
                for k, sq in enumerate(parts):
                    last = mm(dst[:, 0:TOK], ones[:, :], sq, start=(k == 0), stop=(k == len(parts) - 1))
                last.then_inc(s_stat, 1)

            def weight_chunk(dst, slot, src, ready=None, order=range(KC)):
                for n, k in enumerate(order):
                    if ready is not None:
                        pe.wait_ge(ready[0], ready[1] + n + 1)
                    last = mm(dst[:, 0:TOK], w_ring[:, slot, k * P:(k + 1) * P], src[:, k, :],
                              start=(n == 0), stop=(n == KC - 1))
                last.then_inc(s_w_used, 1)

            pe.wait_ge(s_ones, 1)
            pe.wait_ge(s_sq1, 4)
            token_sums(bank[STAT_BANK], [mixedT[:, k, :] for k in range(KC)])
            column_sums(SH1)
            column_sums(SC1)

            for k in range(KC):
                pe.wait_ge(s_w[k % WSLOTS], 16 * (k // WSLOTS + 1))
                pe.wait_ge(s_h, k + 1)
                for t in range(TT):
                    for dst, a, b in ((2 * t, 0, 512), (2 * t + 1, 512, 1024), (4 + t, 1024, QKV)):
                        last = mm(bank[dst][:, 0:b - a], hT[:, k, t * P:(t + 1) * P], w_ring[:, k % WSLOTS, a:b],
                                  start=(k == 0), stop=(k == KC - 1))
                last.then_inc(s_w_used, 1)

            def qk_transpose():
                pe.wait_ge(s_qk, TT)
                pe.wait_ge(s_const, 9)
                for t in range(TT):
                    for pair in range(8):
                        dst = (EVEN_BANK, ODD_BANK, PT_BANK, STAT_BANK)[2 * t + pair // 4]
                        nc.tensor.transpose(bank[dst][:, pair % 4 * P:(pair % 4 + 1) * P],
                                            qS[:, t, pair * P:(pair + 1) * P], ident[:, :])
                for kv in range(NKV):
                    for t in range(TT):
                        at_ = (kv * TT + t) * P
                        last = nc.tensor.transpose(bank[ADA_BANK][:, at_:at_ + P],
                                                   kdup[:, t, kv, :, :].rearrange("p u d -> p (u d)"), ident[:, :])
                last.then_inc(s_qkTps, 1)

            def scores(u):
                t, heads, keys_n = unit_heads(u)
                pe.wait_ge(s_qkT, 5)
                if u:
                    pe.wait_ge(s_scS, 2 * u)
                for i, h in enumerate(heads):
                    o, at_ = h % 2, i % (len(heads) // 2) * keys_n
                    last = mm(bank[(EVEN_BANK, ODD_BANK)[o]][:, at_:at_ + keys_n],
                              qTr[o * HD:(o + 1) * HD, t, h // 2, :],
                              kTr[o * HD:(o + 1) * HD, h // (NQ // NKV), 0:keys_n], start=True, stop=True)
                last.then_inc(s_scps, 1)

            def transpose_probs(u):
                t, heads, keys_n = unit_heads(u)
                nb = keys_n // P
                pr = probs[u % 2][:, 0:len(heads) * (keys_n + 1)].rearrange("p (h k) -> p h k", h=len(heads))
                pe.wait_ge(s_prob, u + 1)
                for b in range(8):
                    if u and b % 4 == 0:
                        pe.wait_ge(s_PT, 2 * (u - 1) + b // 4 + 1)
                    last = nc.tensor.transpose(bank[(PT_BANK, STAT_BANK)[b // 4]][:, b % 4 * P:(b % 4 + 1) * P],
                                               pr[:, b // nb, b % nb * P:(b % nb + 1) * P], ident[:, :])
                    if b % 4 == 3:
                        last.then_inc(s_PTps, 1)

            def values(u):
                t, heads, keys_n = unit_heads(u)
                nb = keys_n // P
                pe.wait_ge(s_PT, 2 * u + 2)
                if u:
                    pe.wait_ge(s_pv, u)
                for i, h in enumerate(heads):
                    o, pair, kv = h % 2, (h - heads[0]) // 2, h // (NQ // NKV)
                    for b in range(nb):
                        last = mm(bank[ADA_BANK][o * HD:(o + 1) * HD, pair * P:(pair + 1) * P],
                                  kvS[:, b, P + kv * HD:P + (kv + 1) * HD],
                                  probsT[u % 2][:, (i * nb + b) * P:(i * nb + b + 1) * P],
                                  start=(b == 0), stop=(b == nb - 1))
                last.then_inc(s_pvps, 1)

            def gates_of(c):
                if c == 0:
                    pe.wait_ge(s_gatew, 16)
                pe.wait_ge(s_conv, c + 1)
                if c:
                    pe.wait_ge(s_gev, 2 * c)
                for gate in range(2):
                    last = mm(bank[GATE_BANK][:, gate * TOK:(gate + 1) * TOK], gate_w[:, gate, c, :],
                              xconv[c % 2], start=True, stop=True)
                last.then_inc(s_gps, 1)

            pe.wait_ge(s_qkvS, 6)
            column_sums(G1)
            for c in range(LC):
                u = c - FIRST_UNIT_CHUNK
                n = KC + 2 * c
                pe.wait_ge(s_w[n % WSLOTS], 16 * (n // WSLOTS + 1))
                if c:
                    pe.wait_ge(s_xev, c)
                weight_chunk(bank[X_BANK], n % WSLOTS, hT)
                if c:
                    gates_of(c - 1)
                if u >= 0:
                    transpose_probs(u)
                n += 1
                pe.wait_ge(s_w[n % WSLOTS], 16 * (n // WSLOTS + 1))
                if c:
                    pe.wait_ge(s_yev, c)
                weight_chunk(bank[Y_BANK], n % WSLOTS, hT)
                if u >= 0:
                    values(u)
                if u == -1:
                    qk_transpose()
                if -1 <= u < UNITS - 1:
                    scores(u + 1)
            gates_of(LC - 1)

            pe.wait_ge(s_pv, UNITS)
            column_sums(SH2)
            pe.wait_ge(s_attnsum, TT + NQ)
            token_sums(bank[STAT_BANK], [attn_sum[:, :]])
            pe.wait_ge(s_lrusum, 1 + LC)
            token_sums(bank[PT_BANK], [lru_sum[:, :]])

            with pe.Fori(0, KC // WSLOTS) as i:
                for j in range(WSLOTS):
                    pe.wait_ge(s_w[j], i * 16 + 16 * (2 * KC // WSLOTS + 1))
                    pe.wait_ge(s_x2, i * WSLOTS + j + 1)
                    weight_chunk(bank[j], j, mixedT, (s_mix, 0) if j == 0 else None, MIX_ORDER)
            column_sums(SC2)
            pe.wait_ge(s_x2add, WSLOTS + KC)
            token_sums(bank[STAT_BANK], [sqsum[:, :]])

            def peer_scores(i, parity):
                head = i * 2 + parity
                first = isinstance(head, int) and head == 0
                for half in range(2):
                    slot = 2 * parity + half
                    pe.wait_ge(s_w[slot], i * 16 + 16 * (3 * KC // WSLOTS + 1))
                    if not first:
                        pe.wait_ge(s_qev, head * 2 + half - 1)
                    weight_chunk(bank[half], slot, hT, (s_h, KC) if first and half == 0 else None)
                if first:
                    pe.wait_ge(s_keys, 16)
                else:
                    pe.wait_ge(s_bests, head)
                for half in range(2):
                    pe.wait_ge(s_qev, head * 2 + half + 1)
                    kt = (keysT[:, half, :] if first else
                          keysT[:, bass.ds(head * 2 + half, 1), :].rearrange("p a n -> p (a n)"))
                    for t in range(TT):
                        at_ = (half * TT + t) * P
                        last = mm(bank[2][:, at_:at_ + P], qpT[half][:, t * P:(t + 1) * P], kt,
                                  start=True, stop=True)
                last.then_inc(s_sps, 1)

            peer_scores(0, 0)
            for n in range(TT * 4):
                t, quarter = divmod(n, 4)
                dst = bank[(3, 4, 5, 7)[n % 4]]
                if n >= 4:
                    pe.wait_ge(s_h2tok, n - 3)
                for k in range(4):
                    last = nc.tensor.transpose(dst[:, k * P:(k + 1) * P],
                                               hT[:, quarter * 4 + k, t * P:(t + 1) * P], ident[:, :])
                last.then_inc(s_h2ps, 1)
            pe.wait_ge(s_h2tok, TT * 4)
            pe.wait_ge(s_brow, 16)
            for n in range(4):
                dst = bank[3 + n]
                mm(dst[:, :], ones[:, :], ada_acc[:, 1, n * 512:(n + 1) * 512], start=True, stop=False)
                mm(dst[:, :], ones[0:1, :], brow[:, n * 512:(n + 1) * 512], start=False, stop=True
                   ).then_inc(s_g2ps, 1)
            peer_scores(0, 1)
            with pe.Fori(1, PH // 2) as i:
                peer_scores(i, 0)
                peer_scores(i, 1)

            pe.wait_ge(s_bests, PH)
            for t in range(TT):
                if t:
                    pe.wait_ge(s_g2, 4)
                for n in range(4):
                    dst = bank[((0, 1, 2, 7), (3, 4, 5, 6))[t][n]]
                    for k in range(4):
                        last = nc.tensor.transpose(dst[:, k * P:(k + 1) * P],
                                                   x2T[:, n * 4 + k, t * P:(t + 1) * P], ident[:, :])
                    last.then_inc(s_x2ps, 1)

        @block.scalar
        def _(act):
            fn = nc.scalar.activation
            own = Chain(act, s_act)
            act.wait_ge(s_cols, 16)
            fn(amp, col("c"), ACT.Tanh, scale=0.5).then_inc(s_silu, 1)
            own.mark(fn(lam_t[0], col("lam"), ACT.Abs))
            own.settle()
            fn(lam_t[0], lam_t[0], ACT.Exp, scale=-1.0).then_inc(s_lamexp, 1)
            act.wait_ge(s_xin, 16)
            for q in range(4):
                fn(mixedT[:, 4 * q:4 * q + 4, :], x2T[:, 4 * q:4 * q + 4, :], ACT.Square).then_inc(s_sq1, 1)
            act.wait_ge(s_ang, 1)
            fn(sin_t, angle, ACT.Sin).then_inc(s_sin, 1)
            fn(cos_t, angle, ACT.Sin, scale=0.5).then_inc(s_sin, 1)

            roots = [0]

            def root(v):
                roots[0] += 1
                act.wait_ge(s_mean, roots[0])
                fn(v, v, ACT.Sqrt).then_inc(s_root, 1)

            def shift(g, base):
                with act.Fori(0, KC) as k:
                    act.wait_ge(s_scaled, k + base + 1)
                    v = hT[:, bass.ds(k, 1), :]
                    fn(v, v, ACT.Identity, bias=ada_col[:, g, bass.ds(k, 1)]).then_inc(s_h, 1)

            root(rinv[:, :])
            act.wait_ge(s_adacol, 1)
            shift(SH1, 0)

            act.wait_ge(s_w_used, KC)
            for t in range(TT):
                for b, dst in ((2 * t, qS[:, t, 0:512]), (2 * t + 1, qS[:, t, 512:1024]), (4 + t, kvS[:, t, :])):
                    fn(dst, bank[b][:, 0:dst.shape[-1]], ACT.Copy).then_inc(s_qkvS, 1)

            def qk_transpose():
                act.wait_ge(s_qkTps, 1)
                for n, b in enumerate((EVEN_BANK, ODD_BANK, PT_BANK, STAT_BANK)):
                    fn(qTr[:, n // 2, n % 2 * 4:n % 2 * 4 + 4, :], bank[b][:, :].rearrange("p (h n) -> p h n", h=4),
                       ACT.Copy).then_inc(s_qkT, 1)
                fn(kTr, bank[ADA_BANK][:, :].rearrange("p (k n) -> p k n", k=NKV), ACT.Copy).then_inc(s_qkT, 1)

            def scores(u):
                _, heads, keys_n = unit_heads(u)
                act.wait_ge(s_shift, u + 1)
                v = probs[u % 2][:, 0:len(heads) * (keys_n + 1)]
                fn(v, v, ACT.Exp).then_inc(s_exp, 1)

            def probs_out(u):
                for b in range(2):
                    act.wait_ge(s_PTps, 2 * u + b + 1)
                    if u >= 2 and b == 0:
                        act.wait_ge(s_pvps, u - 1)
                    fn(probsT[u % 2][:, b * 512:(b + 1) * 512], bank[(PT_BANK, STAT_BANK)[b]][:, :],
                       ACT.Copy).then_inc(s_PT, 1)

            def values_out(u):
                t, heads, _ = unit_heads(u)
                act.wait_ge(s_pvps, u + 1)
                pairs, first = len(heads) // 2, heads[0] // 2
                fn(mixedT[:, LC + first:LC + first + pairs, t * P:(t + 1) * P],
                   bank[ADA_BANK][:, 0:pairs * P].rearrange("p (h n) -> p h n", h=pairs),
                   ACT.Copy).then_inc(s_pv, 1)

            def gates_of(c):
                b = c % 2
                if c == 0:
                    act.wait_ge(s_lam, 1)
                if c >= 2:
                    act.wait_ge(s_lru, c - 1)
                act.wait_ge(s_gps, c + 1)
                fn(th_r[b], bank[GATE_BANK][:, 0:TOK], ACT.Tanh, bias=half_ab[:, c:c + 1], scale=0.5
                   ).then_inc(s_gev, 1)
                fn(th_i[b], bank[GATE_BANK][:, TOK:2 * TOK], ACT.Tanh, bias=half_xb[:, c:c + 1], scale=0.5
                   ).then_inc(s_gev, 1)
                act.wait_ge(s_gev, 2 * c + 1)
                fn(decay[b], th_r[b], ACT.Exp, bias=c4[:, c:c + 1], scale=c4[:, c:c + 1]).then_inc(s_decay, 1)
                fn(drive[b], th_r[b], ACT.Tanh, bias=c4[:, c:c + 1], scale=c4[:, c:c + 1]).then_inc(s_decay, 1)

            def input_scale(c):
                act.wait_ge(s_mag, c + 1)
                fn(drive[c % 2], drive[c % 2], ACT.Sqrt, scale=-1.0).then_inc(s_sqrt, 1)

            for c in range(LC):
                b = c % 2
                u = c - FIRST_UNIT_CHUNK
                if c < TT:
                    act.wait_ge(s_qkms, c + 1)
                    fn(qk_ms, qk_ms, ACT.Sqrt).then_inc(s_qkroot, 1)
                if u >= 0:
                    scores(u)
                act.wait_ge(s_w_used, KC + 2 * c + 1)
                if c >= 2:
                    act.wait_ge(s_conv, c - 1)
                elif c == 0:
                    act.wait_ge(s_const, 9)
                fn(xpad[b][:, 3:3 + TOK], bank[X_BANK][:, 0:TOK], ACT.Copy).then_inc(s_xev, 1)
                if c:
                    gates_of(c - 1)
                if u >= 0:
                    probs_out(u)
                if c:
                    input_scale(c - 1)
                act.wait_ge(s_w_used, KC + 2 * c + 2)
                if c >= 2:
                    act.wait_ge(s_lru, c - 1)
                fn(ysil[b], bank[Y_BANK][:, 0:TOK], ACT.Gelu_apprx_tanh).then_inc(s_yev, 1)
                if u >= 0:
                    values_out(u)
                if u == -1:
                    qk_transpose()
            gates_of(LC - 1)
            input_scale(LC - 1)
            root(sqsum[:, :])
            root(rinv[:, :])

            with act.Fori(0, KC // WSLOTS) as i:
                for j in range(WSLOTS):
                    act.wait_ge(s_x2, i * WSLOTS + j + WSLOTS + 1)
                    act.wait_ge(s_x2add, i * WSLOTS + j + 1)
                    fn(sqb[:, j * TOK:(j + 1) * TOK].unsqueeze(1), x2T[:, bass.ds(i * WSLOTS + j, 1), :], ACT.Square
                       ).then_inc(s_x2sq, 1)
            root(rinv[:, :])
            act.wait_ge(s_adacol, 4)
            shift(SH2, KC)

            def queries(head):
                for half in range(2):
                    act.wait_ge(s_w_used, head * 2 + half + 3 * KC + 1)
                    if half == 0 and not (isinstance(head, int) and head == 0):
                        act.wait_ge(s_sps, head)
                    fn(qpT[half][:, :], bank[half][:, 0:TOK], ACT.Copy).then_inc(s_qev, 1)

            def best_exp(head):
                act.wait_ge(s_bests, head + 1)
                fn(best_e, best_e, ACT.Exp).then_inc(s_bexp, 1)

            def expert_gelu(head, t):
                act.wait_ge(s_row_used, head * (2 * TT * TOPK) + t * 2 * TOPK + TOPK + ROWS)
                fn(gel, dots, ACT.Gelu_apprx_tanh).then_inc(s_gelu, 1)

            queries(0)
            for n in range(TT * 4):
                t, quarter = divmod(n, 4)
                act.wait_ge(s_h2ps, n + 1)
                fn(h2tok[:, t, quarter * 512:(quarter + 1) * 512], bank[(3, 4, 5, 7)[n % 4]][:, :], ACT.Copy
                   ).then_inc(s_h2tok, 1)
            for n in range(4):
                act.wait_ge(s_g2ps, n + 1)
                if n == 0:
                    act.wait_ge(s_g2ps, 4)
                fn(gate2[:, n * 512:(n + 1) * 512], bank[3 + n][:, :], ACT.Copy).then_inc(s_g2, 1)
            best_exp(0)

            def head_step(head, more):
                if more:
                    queries(head + 1)
                expert_gelu(head, 0)
                if more:
                    best_exp(head + 1)
                expert_gelu(head, 1)

            with act.Fori(0, PH - 1) as head:
                head_step(head, True)
            head_step(PH - 1, False)


        @block.vector
        def _(dve):
            v = nc.vector
            own = Chain(dve, s_dve)

            def link(ins):
                own.mark(ins)
                own.settle()

            dve.sem_inc(s_x2, WSLOTS)
            dve.sem_inc(s_row_used, ROWS)
            v.memset(ada_acc[:, 0, :], 0.0).then_inc(s_ada_used, 1)
            v.memset(ada_acc[:, 1, :], 0.0).then_inc(s_ada_used, 1)
            v.memset(ones[:, :], 1.0).then_inc(s_ones, 1)
            for b in range(2):
                own.mark(v.memset(xpad[b][:, 0:3], 0.0))
            for j in range(ROT):
                own.mark(v.memset(invf[:, j:j + 1], float(np.float32(ROPE_THETA ** (-j / ROT)))))
            dve.wait_ge(s_cols, 16)
            dve.wait_ge(s_silu, 1)
            link(v.scalar_tensor_tensor(silu_c, amp, 1.0, col("c"), ALU.add, ALU.mult))
            link(v.tensor_scalar(silu_c, silu_c, 0.5, None, ALU.mult))

            def add_piece(src, acc, k):
                return v.scalar_tensor_tensor(acc, src, silu_c[:, k] if isinstance(k, slice) else
                                              silu_c[:, bass.ds(k, 1)], acc, ALU.mult, ALU.add)

            def ada_group(g):
                with dve.Fori(0, KC // ASLOTS) as i:
                    for j in range(ASLOTS):
                        dve.wait_ge(s_ada[j], i * 16 + 16 * (g * KC // ASLOTS + 1))
                        dve.wait_ge(s_ada_used, i * ASLOTS + j + g * KC + 2)
                        add_piece(ada_ring[:, j, :], ada_acc[:, g % 2, :], i * ASLOTS + j).then_inc(s_ada_used, 1)

            def ada_piece(n):
                g, k = divmod(n, KC)
                if k == 0:
                    dve.wait_ge(s_adaps, g - 1)
                    link(v.memset(ada_acc[:, g % 2, :], 0.0))
                dve.wait_ge(s_ada[n % ASLOTS], 16 * (n // ASLOTS + 1))
                dve.wait_ge(s_ada_used, 2 + n)
                add_piece(ada_ring[:, n % ASLOTS, :], ada_acc[:, g % 2, :], k).then_inc(s_ada_used, 1)

            def ada_column(g):
                dve.wait_ge(s_adaps, g + 1)
                v.tensor_tensor(ada_col[:, g, :], bank[ADA_BANK][:, 0:KC],
                                col("b_ada")[:, g * KC:(g + 1) * KC], ALU.add).then_inc(s_adacol, 1)
                dve.wait_ge(s_adacol, g + 1)

            means = [0]

            def mean(dst, src, n):
                means[0] += 1
                dve.wait_ge(s_stat, means[0])
                v.tensor_scalar(dst, src[:, 0:TOK], 1.0 / n, EPS, ALU.mult, ALU.add).then_inc(s_mean, 1)

            def invert(dst, n):
                dve.wait_ge(s_root, n)
                link(v.reciprocal(dst, dst))

            def modulate(gain, g, base):
                link(v.scalar_tensor_tensor(amp, ada_col[:, g, :], 1.0, col(gain), ALU.add, ALU.mult))
                with dve.Fori(0, KC) as k:
                    v.scalar_tensor_tensor(hT[:, bass.ds(k, 1), :], x2T[:, bass.ds(k, 1), :], amp[:, bass.ds(k, 1)],
                                           rinv[:, :].unsqueeze(1), ALU.mult, ALU.mult).then_inc(s_scaled, 1)

            ada_group(SH1)

            dve.wait_ge(s_pos, 16)
            link(v.tensor_copy(posf, posi))
            for t in range(TT):
                own.mark(v.tensor_scalar(angle[:, t * ROT:(t + 1) * ROT], invf, posf[:, t:t + 1], None, ALU.mult))
            own.settle()
            link(v.tensor_scalar(turns, angle, 1.0 / (2 * math.pi), None, ALU.mult))
            magic = 1.5 * 2.0 ** 23
            link(v.tensor_scalar(turns, turns, magic, None, ALU.add))
            link(v.tensor_scalar(turns, turns, magic, None, ALU.subtract))
            rest = 2 * math.pi
            for bits in (6, 18, None):
                part_ = rest if bits is None else math.floor(rest * 2.0 ** bits) / 2.0 ** bits
                rest -= part_
                link(v.scalar_tensor_tensor(angle, turns, -float(np.float32(part_)), angle, ALU.mult, ALU.add))
            v.tensor_scalar(angle, angle, 3.1415925, -3.1415925, ALU.min, ALU.max).then_inc(s_ang, 1)

            dve.wait_ge(s_lamexp, 1)
            z, zz, s, b1 = lam_t
            link(v.tensor_scalar(zz, z, 2.0, None, ALU.add))
            link(v.reciprocal(zz, zz))
            link(v.tensor_tensor(z, z, zz, ALU.mult))
            link(v.tensor_tensor(zz, z, z, ALU.mult))
            link(v.tensor_scalar(s, zz, 1.0 / 17, None, ALU.mult))
            for odd in (15, 13, 11, 9, 7, 5, 3):
                link(v.scalar_tensor_tensor(s, s, 1.0 / odd, zz, ALU.add, ALU.mult))
            link(v.scalar_tensor_tensor(s, s, 1.0, z, ALU.add, ALU.mult))
            link(v.tensor_scalar(b1, col("lam"), -1.0, 0.0, ALU.mult, ALU.max))
            link(v.scalar_tensor_tensor(s, s, 2.0, b1, ALU.mult, ALU.add))
            own.mark(v.tensor_scalar(half_ab, col("gate_a_b"), 0.5, None, ALU.mult))
            own.mark(v.tensor_scalar(half_xb, col("gate_x_b"), 0.5, None, ALU.mult))
            own.settle()
            v.tensor_scalar(c4, s, -4.0, None, ALU.mult).then_inc(s_lam, 1)

            dve.wait_ge(s_sin, 2)
            link(v.tensor_tensor(cos_t, cos_t, cos_t, ALU.mult))
            link(v.tensor_scalar(cos_t, cos_t, -2.0, 1.0, ALU.mult, ALU.add))

            mean(rinv[:, :], bank[STAT_BANK], D)
            ada_group(SC1)
            invert(rinv[:, :], 1)
            ada_column(SH1)
            ada_column(SC1)
            modulate("norm1_g", SC1, 0)
            link(v.memset(ada_acc[:, G1 % 2, :], 0.0))
            ada_group(G1)

            def qk_norm(t):
                dve.wait_ge(s_qkvS, 3 * (t + 1))
                dve.wait_ge(s_rows, 16)
                q = qS[:, t, :].rearrange("p (h d) -> p h d", h=NQ)
                k = kvS[:, t, 0:P].rearrange("p (h d) -> p h d", h=NKV)
                sq = qk_square.rearrange("p (h d) -> p h d", h=NQK)
                own.mark(v.tensor_tensor(sq[:, 0:NQ, :], q, q, ALU.mult))
                own.mark(v.tensor_tensor(sq[:, NQ:NQK, :], k, k, ALU.mult))
                own.settle()
                link(v.tensor_reduce(qk_ms, sq, AX, ALU.add))
                v.tensor_scalar(qk_ms, qk_ms, 1.0 / HD, EPS, ALU.mult, ALU.add).then_inc(s_qkms, 1)
                dve.wait_ge(s_qkroot, t + 1)
                link(v.reciprocal(qk_ms, qk_ms))
                sides = ((q, NQ, qk_ms[:, 0:NQ], q_gain), (k, NKV, qk_ms[:, NQ:NQK], k_gain))
                for x, n, r, _ in sides:
                    own.mark(v.tensor_tensor(x, x, spread(r, HD, 2), ALU.mult))
                own.settle()
                for x, n, _, gain in sides:
                    own.mark(v.tensor_tensor(x, x, spread(gain, n, 1), ALU.mult))
                own.settle()
                sin, cos = sin_t[:, t * ROT:(t + 1) * ROT], cos_t[:, t * ROT:(t + 1) * ROT]
                places = []
                for x, n, base in ((q, NQ, 0), (k, NKV, 4 * NQ * ROT)):
                    tmp = qk_square[:, base:base + 4 * n * ROT].rearrange("p (a h d) -> p a h d", a=4, h=n)
                    places.append((x, tmp))
                    for a, (half, w) in enumerate(((0, cos), (1, sin), (1, cos), (0, sin))):
                        own.mark(v.tensor_tensor(tmp[:, a], x[:, :, half * ROT:(half + 1) * ROT],
                                                 spread(w, n, 1), ALU.mult))
                own.settle()
                for x, tmp in places:
                    own.mark(v.tensor_tensor(x[:, :, 0:ROT], tmp[:, 0], tmp[:, 1], ALU.subtract))
                    own.mark(v.tensor_tensor(x[:, :, ROT:2 * ROT], tmp[:, 2], tmp[:, 3], ALU.add))
                own.settle()
                for u in range(2):
                    last = v.tensor_copy(kdup[:, t, :, u, :], k)
                    if u == 0:
                        own.mark(last)
                own.settle()
                last.then_inc(s_qk, 1)

            def softmax(u):
                t, heads, keys_n = unit_heads(u)
                n = len(heads)
                pr = probs[u % 2][:, 0:n * (keys_n + 1)].rearrange("p (h k) -> p h k", h=n)
                if u >= 2:
                    dve.wait_ge(s_PTps, 2 * (u - 1))
                for o in range(2):
                    own.mark(v.tensor_copy(pr[:, o * n // 2:(o + 1) * n // 2, keys_n:keys_n + 1],
                                           sink[:, heads[0] + o:heads[0] + n:2].unsqueeze(2)))
                dve.wait_ge(s_scps, u + 1)
                for o, b in enumerate((EVEN_BANK, ODD_BANK)):
                    v.scalar_tensor_tensor(pr[:, o * n // 2:(o + 1) * n // 2, 0:keys_n],
                                           bank[b][:, :].rearrange("p (h k) -> p h k", h=n // 2), HD ** -0.5,
                                           spread(mask[t], n // 2, 1), ALU.mult, ALU.add).then_inc(s_scS, 1)
                own.settle()
                dve.wait_ge(s_scS, 2 * u + 2)
                link(v.tensor_reduce(mx[:, 0:n], pr, AX, ALU.max))
                v.tensor_tensor(pr, pr, spread(mx[:, 0:n], keys_n + 1, 2), ALU.subtract).then_inc(s_shift, 1)
                mid_piece()
                dve.wait_ge(s_exp, u + 1)
                link(v.tensor_reduce(den[:, 0:n], pr, AX, ALU.add))
                link(v.reciprocal(den[:, 0:n], den[:, 0:n]))
                v.tensor_tensor(pr[:, :, 0:keys_n], pr[:, :, 0:keys_n], spread(den[:, 0:n], keys_n, 2),
                                ALU.mult).then_inc(s_prob, 1)

            pieces = iter(range(3 * KC, ADA_GROUPS * KC))

            def mid_piece():
                for n in itertools.islice(pieces, 1):
                    ada_piece(n)

            def convolve(c):
                b = c % 2
                dve.wait_ge(s_xev, c + 1)
                if c >= 2:
                    dve.wait_ge(s_gps, c - 1)
                taps = [colv[:, COLS["conv_w"][0] + k * LC + c:COLS["conv_w"][0] + k * LC + c + 1] for k in range(4)]
                link(v.tensor_scalar(xconv[b], xpad[b][:, 0:TOK], taps[0], col("conv_b", c), ALU.mult, ALU.add))
                for k in range(1, 4):
                    ins = v.scalar_tensor_tensor(xconv[b], xpad[b][:, k:k + TOK], taps[k], xconv[b],
                                                 ALU.mult, ALU.add)
                    if k < 3:
                        link(ins)
                ins.then_inc(s_conv, 1)

            def magnitude(c):
                b = c % 2
                dve.wait_ge(s_decay, 2 * c + 2)
                link(v.tensor_tensor(bscan, decay[b], decay[b], ALU.mult))
                v.scalar_tensor_tensor(drive[b], bscan, 1.0, drive[b], ALU.add, ALU.mult).then_inc(s_mag, 1)
                dve.wait_ge(s_mag, c + 1)
                link(v.scalar_tensor_tensor(bscan, th_i[b], 1.0, xconv[b], ALU.add, ALU.mult))

            def recurrence(c):
                b = c % 2
                dve.wait_ge(s_sqrt, c + 1)
                link(v.scalar_tensor_tensor(bscan, bscan, 0.5, drive[b], ALU.mult, ALU.mult))
                link(v.tensor_tensor_scan(mixedT[:, c, :], decay[b], bscan, 0.0, ALU.mult, ALU.add))
                dve.wait_ge(s_yev, c + 1)
                v.tensor_tensor(mixedT[:, c, :], mixedT[:, c, :], ysil[b], ALU.mult).then_inc(s_lru, 1)

            ada_column(G1)
            for c in range(LC):
                u = c - FIRST_UNIT_CHUNK
                if c < TT:
                    qk_norm(c)
                    mid_piece()
                if u >= 0:
                    softmax(u)
                convolve(c)
                if c:
                    magnitude(c - 1)
                mid_piece()
                if c:
                    recurrence(c - 1)
                mid_piece()
            magnitude(LC - 1)
            recurrence(LC - 1)

            mean(sqsum[:, :], bank[STAT_BANK], LRU)
            mean(rinv[:, :], bank[PT_BANK], LRU)
            ada_column(SH2)
            invert(sqsum[:, :], 2)
            for k in MIX_ORDER:
                if k == 0:
                    invert(rinv[:, :], 3)
                v.scalar_tensor_tensor(mixedT[:, k, :], mixedT[:, k, :], col("out_g", k),
                                       (rinv if k < LC else sqsum)[:, :], ALU.mult, ALU.mult).then_inc(s_mix, 1)
            for c in range(KC):
                dve.wait_ge(s_w_used, 2 * KC + c + 1)
                v.scalar_tensor_tensor(x2T[:, c, :], bank[c % WSLOTS][:, 0:TOK], ada_col[:, G1, c:c + 1],
                                       x2T[:, c, :], ALU.mult, ALU.add).then_inc(s_x2, 1)
                for _ in range(1 + c % 2):
                    mid_piece()
            ada_column(SC2)
            mean(rinv[:, :], bank[STAT_BANK], D)
            invert(rinv[:, :], 4)
            dve.wait_ge(s_x2, WSLOTS + KC)
            modulate("norm2_g", SC2, KC)

            def top16(values_, src, at_):
                for j in range(len(src)):
                    own.mark(v.max(values_[j][:, 0:8], src[j]))
                own.settle()
                for j in range(len(src)):
                    own.mark(v.max_index(at_[j][:, 0:8], values_[j][:, 0:8], src[j]))
                own.settle()
                for j in range(len(src)):
                    own.mark(v.match_replace(src[j], values_[j][:, 0:8], src[j], GONE))
                own.settle()
                for j in range(len(src)):
                    own.mark(v.max(values_[j][:, 8:16], src[j]))
                own.settle()
                for j in range(len(src)):
                    own.mark(v.max_index(at_[j][:, 8:16], values_[j][:, 8:16], src[j]))
                own.settle()

            def select(head, parity):
                dve.wait_ge(s_sps, head + 1)
                link(v.tensor_copy(sc_s, bank[2][:, :]))
                sets = [(a, t) for a in range(2) for t in range(TT)]
                top16([top_v[:, a, t, :] for a, t in sets],
                      [sc_s[:, (a * TT + t) * NKEY:(a * TT + t + 1) * NKEY] for a, t in sets],
                      [top_i[:, a, t, :] for a, t in sets])
                own.mark(v.tensor_scalar(top_f[:, 0], top_i[:, 0], float(NKEY), None, ALU.mult))
                own.mark(v.tensor_copy(top_f[:, 1], top_i[:, 1]))
                own.settle()
                off = 0
                for i0, r, n in RECTS:
                    for dst, src in ((cand_s, top_v), (cand_i, top_f)):
                        own.mark(v.tensor_tensor(
                            dst[:, :, off:off + r * n].rearrange("p t (r n) -> p t r n", r=r),
                            spread(src[:, 0, :, i0:i0 + r], n, 3), spread(src[:, 1, :, 0:n], r, 2), ALU.add))
                    off += r * n
                own.settle()
                top16([best_v[:, t, :] for t in range(TT)], [cand_s[:, t, :] for t in range(TT)],
                      [best_p[:, t, :] for t in range(TT)])
                v.tensor_tensor(best_e, best_v, best_v[:, :, 0:1].broadcast_to([P, TT, TOPK]), ALU.subtract
                                ).then_inc(s_bests, 1)
                link(v.tensor_copy(best_f, best_p))
                for t in range(TT):
                    link(v.tensor_tensor(hot, spread(best_f[:, t, :], NCAND, 2), spread(iota_c, TOPK, 1),
                                         ALU.is_equal))
                    link(v.tensor_tensor(hot, hot, spread(cand_i[:, t, :], TOPK, 1), ALU.mult))
                    link(v.tensor_reduce(best_v[:, t, :], hot, AX, ALU.add))
                v.tensor_copy(idx[parity], best_v.rearrange("p t k -> p (t k)")).then_inc(s_idx, 1)
                dve.wait_ge(s_bexp, head + 1)
                link(v.tensor_reduce(tksum, best_e, AX, ALU.add))
                link(v.reciprocal(tksum, tksum))
                link(v.tensor_tensor(gsm[parity].rearrange("p (t k) -> p t k", t=TT), best_e,
                                     spread(tksum, TOPK, 2), ALU.mult))

            def experts(i, parity, t):
                base = (parity * TT + t) * 2 * TOPK
                for k in range(TOPK):
                    local = base + k
                    dve.wait_ge(s_row[local % ROWS], i * (16 * PAIR_ROWS // ROWS) + 16 * (local // ROWS + 1))
                    v.tensor_tensor_reduce(ring_row(local % ROWS), ring_row(local % ROWS), h2tok[:, t, :], 1.0, 0.0,
                                           ALU.mult, ALU.add, dots[:, k:k + 1]).then_inc(s_row_used, 1)
                dve.wait_ge(s_gelu, i * 2 * TT + parity * TT + t + 1)
                link(v.tensor_tensor(wgt, gel, gsm[parity][:, t * TOPK:(t + 1) * TOPK], ALU.mult))
                for k in range(TOPK):
                    local = base + TOPK + k
                    dve.wait_ge(s_row[local % ROWS], i * (16 * PAIR_ROWS // ROWS) + 16 * (local // ROWS + 1))
                    dve.wait_ge(s_row_used, i * PAIR_ROWS + local + ROWS)
                    v.scalar_tensor_tensor(peer[:, t, :], ring_row(local % ROWS), wgt[:, k:k + 1], peer[:, t, :],
                                           ALU.mult, ALU.add).then_inc(s_row_used, 1)

            def head_pair(i, more):
                experts(i, 0, 0)
                select(i * 2 + 1, 1)
                experts(i, 0, 1)
                experts(i, 1, 0)
                if more:
                    select(i * 2 + 2, 0)
                experts(i, 1, 1)

            dve.wait_ge(s_const, 10)
            select(0, 0)
            dve.wait_ge(s_h2tok, TT * 4)
            own.restart()
            with dve.Fori(0, PH // 2 - 1) as i:
                head_pair(i, True)
                own.restart()
            head_pair(PH // 2 - 1, False)

            dve.wait_ge(s_g2, 4)
            dve.wait_ge(s_row_used, ROWS + PH * TT * 2 * TOPK)
            for t in range(TT):
                for n in range(4):
                    part_, c = peer[:, t, n * 512:(n + 1) * 512], 4 * t + n
                    link(v.tensor_tensor(part_, part_, gate2[:, n * 512:(n + 1) * 512], ALU.mult))
                    dve.wait_ge(s_x2ps, c + 1)
                    v.tensor_tensor(part_, part_, bank[((0, 1, 2, 7), (3, 4, 5, 6))[t][n]][:, :], ALU.add
                                    ).then_inc(s_fin, 1)


def kernel(**inputs):
    import concourse.bacc as bacc
    from concourse.bass_utils import run_bass_kernel_spmd

    a = {n: np.asarray(x) for n, x in inputs.items()}

    def columns(v):
        return v.reshape(-1, P).T

    w_in, depth = a["w_in"][0], 0
    halves = w_in[:, 0:2 * LRU].reshape(KC, P, 2, LC, P)

    def chunks(w):
        return w.reshape(KC, P, -1, P).transpose(2, 1, 0, 3).reshape(-1, P, D)

    arrays = {
        "xT": a["x"][0].T.reshape(KC, P, TOK).transpose(1, 0, 2).reshape(P, KC * TOK),
        "cols": np.concatenate([columns(a[n][0]) for n in ("c", "b_ada", "norm1_g", "norm2_g")]
                               + [columns(a["out_norm_lru_g"][0]), columns(a["out_norm_attn_g"][0])]
                               + [columns(a[n][0]) for n in ("conv_w", "conv_b", "lru_gate_a_b", "lru_gate_x_b",
                                                             "lru_lambda")], axis=1),
        "rowv": np.broadcast_to(np.concatenate([a["q_norm_g"][0], a["k_norm_g"][0], a["attn_sinks"][0]]), (P, NROWV)),
        "pos": a["positions"][0].reshape(TT, P).T,
        "w_ada": a["w_ada"][0].reshape(KC, P, ADA_GROUPS, D).transpose(2, 0, 1, 3).reshape(ADA_GROUPS * KC, P, D),
        "b_gate2": a["b_ada"][:, 5 * D:],
        "w_qkv": w_in[:, 2 * LRU:].reshape(KC, P, QKV),
        "w_chunks": np.concatenate([halves.transpose(3, 2, 1, 0, 4).reshape(KC, P, D), chunks(a["w_out"][0]),
                                    chunks(a["peer_w_q"][0])]),
        "gates": np.stack([a["lru_gate_a_w"][0], a["lru_gate_x_w"][0]]).transpose(2, 0, 1, 3).reshape(P, 2 * LC * P),
        "keys": a["peer_sub_keys"][0].transpose(3, 0, 1, 2).reshape(P, 2 * PH * NKEY),
        "peer_u": a["peer_u"][0],
        "peer_v": a["peer_v"][0],
    }
    nc = bacc.Bacc("TRN2", target_bir_lowering=False, num_devices=1)
    sent, args = {}, []
    for name, x in arrays.items():
        x = np.ascontiguousarray(x)
        sent[f"in_{name}"] = x
        args.append(nc.dram_tensor(f"in_{name}", x.shape, mybir.dt.from_np(x.dtype), kind="ExternalInput").ap())
    result = nc.dram_tensor("result", (TOK, D), F32, kind="ExternalOutput").ap()
    build(nc, *args, result)
    r = run_bass_kernel_spmd(nc, [sent], core_ids=[0])
    return r.results[0]["result"].reshape(1, TOK, D)
```

```python
import itertools
import math
from contextlib import ExitStack

import numpy as np

import concourse.bass as bass
from concourse import mybir

P = 128
D = 2048
TOK = 256
KC = D // P
TT = TOK // P
LRU = 1024
LC = LRU // P
HD = 64
NQ, NKV = 16, 2
NQK = NQ + NKV
QKV = (NQ + 2 * NKV) * HD
ROT = 8
ROPE_THETA = 500000.0
PH = 8
NKEY = 128
TOPK = 16
EPS = 1e-6
ADA_GROUPS = 6
SH1, SC1, G1, SC2, SH2, G2 = range(ADA_GROUPS)
ADA_PARTS = (0, 1, 2, 4, 3, 5)
NEG = -1e30
GONE = -3e38

RECTS = [(0, 1, 16), (1, 1, 8), (2, 2, 5), (4, 4, 3), (8, 8, 1)]
NCAND = sum(r * c for _, r, c in RECTS)

WSLOTS = 4
ASLOTS = 4
ROWS = 8
PAIR_ROWS = 2 * TT * 2 * TOPK

COLS = {}
_at = 0
for _name, _n in (("c", KC), ("b_ada", ADA_GROUPS * KC), ("norm1_g", KC), ("norm2_g", KC), ("out_g", KC),
                  ("conv_w", 4 * LC), ("conv_b", LC), ("gate_a_b", LC), ("gate_x_b", LC), ("lam", LC)):
    COLS[_name] = (_at, _at + _n)
    _at += _n
NCOLS = _at
SMALL = 560
NROWV = 2 * HD + NQ

ALU = mybir.AluOpType
ACT = mybir.ActivationFunctionType
AX = mybir.AxisListType.X
F32 = mybir.dt.float32
I32 = mybir.dt.int32
U32 = mybir.dt.uint32


class Chain:

    def __init__(self, engine, sem):
        self.engine, self.sem, self.count = engine, sem, 0

    def mark(self, ins):
        ins.then_inc(self.sem, 1)
        self.count += 1

    def settle(self):
        if self.count:
            self.engine.wait_ge(self.sem, self.count)

    def restart(self):
        self.settle()
        self.engine.sem_clear(self.sem)
        self.count = 0


def pairs_before(u):
    return sum(len(unit_heads(w)[1]) // 2 for w in range(u))


def unit_heads(u):
    t, first, n = (0, 8 * u, 8) if u < 2 else (1, 4 * (u - 2), 4)
    heads = list(range(first, first + n, 2)) + list(range(first + 1, first + n, 2))
    return t, heads, P * (t + 1)


MIX_ORDER = list(range(LC, 2 * LC)) + list(range(LC))
UNITS = 6
FIRST_UNIT_CHUNK = 2


def build(nc, xT, cols, rowv, pos, w_ada, w_qkv, w_chunks, gates, keys, peer_u, peer_v, out):
    with ExitStack() as ctx:
        def sb(name, shape, dt=F32):
            return ctx.enter_context(nc.sbuf_tensor(name, shape, dt))

        def sem(name):
            return ctx.enter_context(nc.semaphore(name))

        x2T = sb("x2T", [P, KC, TOK])
        h_wide = sb("h_wide", [P, KC, TOK + 1])
        hT = h_wide[:, :, 0:TOK]
        mixedT = sb("mixedT", [P, KC, TOK])
        h2tok = mixedT[:, :, :].rearrange("p a b -> p (a b)").rearrange("p (t d) -> p t d", t=TT)
        peer = sb("peer", [P, TT, D])
        w_ring = sb("w_ring", [P, WSLOTS, D])
        ada_ring = sb("ada_ring", [P, ASLOTS, D])
        silu_row = sb("silu_row", [P, D])
        picks = sb("picks", [P, D])
        keysT = sb("keysT", [P, 2 * PH, NKEY])
        mixer = sb("mixer", [P, 6 * D])
        colv = sb("colv", [P, NCOLS])
        rows = sb("rows", [P, NROWV])
        ident = sb("ident", [P, P])
        ones = sb("ones", [P, P])
        small = sb("small", [P, SMALL])

        peer_flat = peer[:, :, :].rearrange("p t d -> p (t d)")
        gate_w = peer_flat[:, 0:2048].rearrange("p (g c n) -> p g c n", g=2, c=LC)
        qS = peer_flat[:, 2048:4096].rearrange("p (t q) -> p t q", t=TT)

        cut = [0]

        def part(n):
            cut[0] += n
            assert cut[0] <= 6 * D
            return mixer[:, cut[0] - n:cut[0]]

        kvS = part(512).rearrange("p (t n) -> p t n", t=TT)
        kdup = part(512).rearrange("p (t k u d) -> p t k u d", t=TT, k=NKV, u=2)
        qTr = part(2048).rearrange("p (t h n) -> p t h n", t=TT, h=8)
        kTr = part(512).rearrange("p (k n) -> p k n", k=NKV)
        probs = [part(8 * 129) for _ in range(2)]
        probsT = [part(1024) for _ in range(2)]
        qk_square = mixer[:, cut[0] - 2048 - 2 * 8 * 129:cut[0] - 2048 - 2 * 8 * 129 + NQK * HD]
        xpad = [part(260) for _ in range(2)]
        xconv = [part(TOK) for _ in range(2)]
        th_r = [part(TOK) for _ in range(2)]
        th_i = [part(TOK) for _ in range(2)]
        decay = [part(TOK) for _ in range(2)]
        drive = [part(TOK) for _ in range(2)]
        ysil = [part(TOK) for _ in range(2)]
        bscan = part(TOK)

        def ring_row(slot):
            if slot < 6:
                return mixer[:, slot * D:(slot + 1) * D]
            return ada_ring[:, ASLOTS - 2 + slot - 6, :]

        mask = [part(P), part(2 * P)]
        attn_sq = part(P)
        lru_sq = sb("lru_sq", [P, TOK])
        rinv = sb("rinv", [P, TOK])
        sqsum = sb("sqsum", [P, TOK])
        lru_sum, attn_sum = rinv, sqsum
        qpT = [sqsum, lru_sq]
        x2_squares = probs[0]
        last_sq = probsT[0][:, 0:2 * TOK]

        at = [0]

        def little(n, dt=F32):
            at[0] += n
            assert at[0] <= SMALL
            v = small[:, at[0] - n:at[0]]
            return v if dt == F32 else v.bitcast(dt)

        silu_c = little(KC)
        ada_col = little(ADA_GROUPS * KC).rearrange("p (g k) -> p g k", g=ADA_GROUPS)
        ada_dot = little(ASLOTS)
        amp = little(KC)
        c4 = little(LC)
        half_ab = little(LC)
        half_xb = little(LC)
        angle = little(TT * ROT)
        turns = little(TT * ROT)
        sin_t = little(TT * ROT)
        cos_t = little(TT * ROT)
        invf = little(ROT)
        posf = little(TT)
        posi = little(TT, I32)
        qk_ms = little(NQK)
        neg_max = little(8)
        den = little(8)
        lam_t = [little(LC) for _ in range(4)]
        iota_c = little(NCAND)
        idx = [little(TT * TOPK, U32) for _ in range(2)]
        gsm = [little(TT * TOPK) for _ in range(2)]
        dots = little(TOPK)
        gel = little(TOPK)
        wgt = little(TOPK)
        tick = little(ROWS + 1)
        tksum = little(TT)
        query_shift = little(2)

        tk = [0]

        def topk_part(n, dt=F32):
            tk[0] += n
            assert tk[0] <= D
            v = picks[:, tk[0] - n:tk[0]]
            return v if dt == F32 else v.bitcast(dt)

        sc_s = topk_part(2 * TT * NKEY)
        top_v = topk_part(2 * TT * TOPK).rearrange("p (a t k) -> p a t k", a=2, t=TT)
        top_i = topk_part(2 * TT * TOPK, U32).rearrange("p (a t k) -> p a t k", a=2, t=TT)
        top_f = topk_part(2 * TT * TOPK).rearrange("p (a t k) -> p a t k", a=2, t=TT)
        cand_s = topk_part(TT * NCAND).rearrange("p (t c) -> p t c", t=TT)
        cand_i = topk_part(TT * NCAND).rearrange("p (t c) -> p t c", t=TT)
        best_v = topk_part(TT * TOPK).rearrange("p (t k) -> p t k", t=TT)
        best_p = topk_part(TT * TOPK, U32).rearrange("p (t k) -> p t k", t=TT)
        best_e = topk_part(TT * TOPK).rearrange("p (t k) -> p t k", t=TT)
        best_f = topk_part(TT * TOPK).rearrange("p (t k) -> p t k", t=TT)
        hot = topk_part(TOPK * NCAND).rearrange("p (k c) -> p k c", k=TOPK)
        gate2 = picks[:, :]

        bank = [ctx.enter_context(nc.psum_tensor(f"bank{i}", [P, 512], F32)) for i in range(8)]
        X_BANK, Y_BANK, GATE_BANK, EVEN_BANK, ODD_BANK, PT_BANK, PV_BANK, STAT_BANK = range(8)

        s_cols, s_xin, s_rows, s_pos, s_gatew, s_keys = map(
            sem, ("s_cols", "s_xin", "s_rows", "s_pos", "s_gatew", "s_keys"))
        s_w = [sem(f"s_w{i}") for i in range(WSLOTS)]
        s_wx = [sem(f"s_wx{i}") for i in range(2)]
        s_w_used = sem("s_w_used")
        s_ada = [sem(f"s_ada{i}") for i in range(ASLOTS)]
        s_ada_used = sem("s_ada_used")
        s_ident = sem("s_ident")
        s_silups, s_silurow = sem("s_silups"), sem("s_silurow")
        s_const = sem("s_const")
        s_ones = sem("s_ones")
        s_dve, s_act = sem("s_dve"), sem("s_act")
        s_silu = sem("s_silu")
        s_sq1 = sem("s_sq1")
        s_stat, s_mean, s_root = sem("s_stat"), sem("s_mean"), sem("s_root")
        s_shift1, s_scale1, s_adacol = sem("s_shift1"), sem("s_scale1"), sem("s_adacol")
        s_amp = sem("s_amp")
        s_inv = sem("s_inv")
        s_scaled = sem("s_scaled")
        s_h = sem("s_h")
        s_h2 = sem("s_h2")
        s_qkvS = sem("s_qkvS")
        s_ang, s_sin = sem("s_ang"), sem("s_sin")
        s_lamexp, s_lam = sem("s_lamexp"), sem("s_lam")
        s_qkms, s_qkroot, s_qk = sem("s_qkms"), sem("s_qkroot"), sem("s_qk")
        s_qkTps, s_qkT = sem("s_qkTps"), sem("s_qkT")
        s_gps = sem("s_gps")
        s_xev, s_tap, s_conv, s_yev, s_gev = sem("s_xev"), sem("s_tap"), sem("s_conv"), sem("s_yev"), sem("s_gev")
        s_decay, s_mag, s_sqrt, s_lru = sem("s_decay"), sem("s_mag"), sem("s_sqrt"), sem("s_lru")
        s_scps, s_scS, s_shift, s_exp, s_prob = (
            sem("s_scps"), sem("s_scS"), sem("s_shift"), sem("s_exp"), sem("s_prob"))
        s_PTps, s_PT, s_pvps, s_pv = sem("s_PTps"), sem("s_PT"), sem("s_pvps"), sem("s_pv")
        s_mix = sem("s_mix")
        s_lastsq = sem("s_lastsq")
        s_lrusq, s_lrusum, s_attnsq, s_attnsum = sem("s_lrusq"), sem("s_lrusum"), sem("s_attnsq"), sem("s_attnsum")
        s_x2, s_x2sq, s_x2add, s_shift2 = sem("s_x2"), sem("s_x2sq"), sem("s_x2add"), sem("s_shift2")
        s_qev, s_sps = sem("s_qev"), sem("s_sps")
        s_h2ps, s_h2tok = sem("s_h2ps"), sem("s_h2tok")
        s_bests, s_bexp, s_idx = sem("s_bests"), sem("s_bexp"), sem("s_idx")
        s_row = [sem(f"s_row{i}") for i in range(ROWS)]
        s_row_used = sem("s_row_used")
        s_hold = sem("s_hold")
        s_gelu = sem("s_gelu")
        s_g2ps, s_g2 = sem("s_g2ps"), sem("s_g2")
        s_x2ps, s_fin, s_out = sem("s_x2ps"), sem("s_fin"), sem("s_out")

        def col(name, k=None):
            a, b = COLS[name]
            return colv[:, a:b] if k is None else colv[:, a + k:a + k + 1]

        q_gain, k_gain, sink = rows[:, 0:HD], rows[:, HD:2 * HD], rows[:, 2 * HD:2 * HD + NQ]

        def spread(ap, n, axis):
            wide = ap.unsqueeze(axis)
            shape = list(wide.shape)
            shape[axis] = n
            return wide.broadcast_to(shape)

        def piece(stack, n):
            return stack[bass.ds(n, 1)].rearrange("a p n -> (a p) n")

        block = ctx.enter_context(nc.Block())

        @block.sync
        def _(sp):
            sp.dma_start(colv[:, :], cols).then_inc(s_cols, 16)
            sp.dma_start(posi, pos).then_inc(s_pos, 16)
            sp.dma_start(rows[:, :], rowv).then_inc(s_rows, 16)
            sp.dma_start(x2T[:, :, :], xT.rearrange("p (k t) -> p k t", k=KC)).then_inc(s_xin, 16)
            for j in range(WSLOTS):
                for n in (2 * j, 2 * j + 1):
                    if n >= ASLOTS:
                        sp.wait_ge(s_ada_used, n - ASLOTS + 1)
                    sp.dma_start(ada_ring[:, n % ASLOTS, :], w_ada[n]).then_inc(s_ada[n % ASLOTS], 16)
                sp.dma_start(w_ring[:, j, 0:QKV], w_qkv[j]).then_inc(s_w[j], 16)
            with sp.Fori(1, KC // WSLOTS) as i:
                for j in range(WSLOTS):
                    for n in (2 * j, 2 * j + 1):
                        sp.wait_ge(s_ada_used, i * 2 * ASLOTS + n - ASLOTS + 1)
                        sp.dma_start(ada_ring[:, n % ASLOTS, :], piece(w_ada, i * 2 * ASLOTS + n)
                                     ).then_inc(s_ada[n % ASLOTS], 16)
                    sp.wait_ge(s_w_used, i * WSLOTS + j - WSLOTS + 1)
                    sp.dma_start(w_ring[:, j, 0:QKV], piece(w_qkv, i * WSLOTS + j)).then_inc(s_w[j], 16)
            sp.dma_start(gate_w, gates.rearrange("p (g c n) -> p g c n", g=2, c=LC)).then_inc(s_gatew, 16)
            with sp.Fori(0, 4) as i:
                for j in range(16):
                    if j % 2 == 0:
                        sp.wait_ge(s_w_used, KC + i * 8 + j // 2 - WSLOTS + 1)
                        sp.dma_start(w_ring[:, j // 2 % WSLOTS, :], piece(w_chunks, i * 8 + j // 2)
                                     ).then_inc(s_w[j // 2 % WSLOTS], 16)
                    sp.wait_ge(s_ada_used, 2 * KC + i * 16 + j - ASLOTS + 1)
                    sp.dma_start(ada_ring[:, j % ASLOTS, :], piece(w_ada, 2 * KC + i * 16 + j)
                                 ).then_inc(s_ada[j % ASLOTS], 16)
            for j in range(WSLOTS):
                sp.wait_ge(s_w_used, 3 * KC + j - WSLOTS + 1)
                sp.dma_start(w_ring[:, j, :], w_chunks[2 * KC + j]).then_inc(s_w[j], 16)
                if j == 1:
                    sp.dma_start(keysT[:, :, :], keys.rearrange("p (c n) -> p c n", c=2 * PH)).then_inc(s_keys, 16)
            for j in range(2):
                sp.wait_ge(s_ada_used, ADA_GROUPS * KC - ASLOTS + j + 1)
                sp.dma_start(ada_ring[:, j, :], w_chunks[2 * KC + WSLOTS + j]).then_inc(s_wx[j], 16)
            for j in range(KC - WSLOTS - 2):
                sp.wait_ge(s_w_used, 3 * KC + (j if j < WSLOTS else j + 2) + 1)
                sp.dma_start(w_ring[:, j % WSLOTS, :], w_chunks[2 * KC + WSLOTS + 2 + j]
                             ).then_inc(s_w[j % WSLOTS], 16)
            for t in range(TT):
                for n in range(4):
                    sp.wait_ge(s_fin, 4 * t + n + 1)
                    sp.dma_start(out[t * P:(t + 1) * P, n * 512:(n + 1) * 512], peer[:, t, n * 512:(n + 1) * 512]
                                 ).then_inc(s_out, 16)
            sp.wait_ge(s_out, 16 * TT * 4)

        @block.gpsimd
        def _(pool):
            g = nc.gpsimd
            g.memset(ident[:, :], 0.0).then_inc(s_const, 1)
            pool.wait_ge(s_const, 1)
            g.affine_select(out=ident[:, :], in_=ident[:, :], compare_op=ALU.not_equal, fill=1.0, base=0,
                            pattern=[[-1, P]], channel_multiplier=1).then_inc(s_ident, 1)
            g.memset(mask[0], 0.0).then_inc(s_const, 1)
            g.memset(mask[1], 0.0).then_inc(s_const, 1)
            g.memset(tick[:, ROWS:ROWS + 1], 0.0).then_inc(s_const, 1)
            g.memset(tick[:, 0:ROWS], 0.0).then_inc(s_hold, ROWS)
            g.iota(iota_c, pattern=[[1, NCAND]], base=0, channel_multiplier=0,
                   allow_small_or_imprecise_dtypes=True).then_inc(s_const, 1)
            pool.wait_ge(s_const, 5)
            g.affine_select(out=mask[0], in_=mask[0], compare_op=ALU.is_ge, fill=NEG, base=0,
                            pattern=[[-1, P]], channel_multiplier=1).then_inc(s_const, 1)
            g.affine_select(out=mask[1][:, 0:P], in_=mask[1][:, 0:P], compare_op=ALU.is_ge, fill=NEG, base=-1,
                            pattern=[[1, P]], channel_multiplier=-1).then_inc(s_const, 1)
            g.affine_select(out=mask[1][:, P:2 * P], in_=mask[1][:, P:2 * P], compare_op=ALU.is_ge, fill=NEG,
                            base=0, pattern=[[-1, P]], channel_multiplier=1).then_inc(s_const, 1)
            pool.wait_ge(s_xin, 16)
            pool.wait_ge(s_inv, 1)
            with pool.Fori(0, KC) as k:
                g.tensor_tensor(hT[:, bass.ds(k, 1), :], x2T[:, bass.ds(k, 1), :], rinv[:, :].unsqueeze(1), ALU.mult
                                ).then_inc(s_scaled, 1)
            pool.wait_ge(s_scaled, KC)
            g.memset(lru_sum[:, :], 0.0).then_inc(s_lrusum, 1)
            g.memset(attn_sum[:, :], 0.0).then_inc(s_attnsum, TT)
            for c in range(LC - 1):
                pool.wait_ge(s_lru, c + 1)
                pool.wait_ge(s_lrusum, c + 1)
                g.tensor_tensor(lru_sq[:, :], mixedT[:, c, :], mixedT[:, c, :], ALU.mult).then_inc(s_lrusq, 1)
                pool.wait_ge(s_lrusq, c + 1)
                g.tensor_tensor(lru_sum[:, :], lru_sum[:, :], lru_sq[:, :], ALU.add).then_inc(s_lrusum, 1)
                u = c - FIRST_UNIT_CHUNK
                if u >= 0:
                    t, heads, _ = unit_heads(u)
                    pool.wait_ge(s_pv, u + 1)
                    for pair in range(heads[0] // 2, heads[0] // 2 + len(heads) // 2):
                        o = mixedT[:, LC + pair, t * P:(t + 1) * P]
                        done_ = pairs_before(u) + pair - heads[0] // 2
                        pool.wait_ge(s_attnsum, TT + done_)
                        g.tensor_tensor(attn_sq[:, :], o, o, ALU.mult).then_inc(s_attnsq, 1)
                        pool.wait_ge(s_attnsq, done_ + 1)
                        sum_ = attn_sum[:, t * P:(t + 1) * P]
                        g.tensor_tensor(sum_, sum_, attn_sq[:, :], ALU.add).then_inc(s_attnsum, 1)
            pool.wait_ge(s_mix, KC)
            g.memset(sqsum[:, :], 0.0).then_inc(s_x2add, WSLOTS)
            g.memset(peer[:, :, :], 0.0).then_inc(s_const, 1)
            with pool.Fori(0, KC // WSLOTS) as i:
                for j in range(WSLOTS):
                    pool.wait_ge(s_x2sq, i * WSLOTS + j + 1)
                    pool.wait_ge(s_x2add, i * WSLOTS + j + WSLOTS)
                    g.tensor_tensor(sqsum[:, :], sqsum[:, :], x2_squares[:, j * TOK:(j + 1) * TOK],
                                    ALU.add).then_inc(s_x2add, 1)
            pool.wait_ge(s_inv, 4)
            pool.wait_ge(s_w_used, 3 * KC + 2)
            for k in range(KC):
                g.tensor_tensor(hT[:, k, :], hT[:, k, :], rinv[:, :], ALU.mult).then_inc(s_scaled, 1)
            with pool.Fori(0, PH // 2) as i:
                for local in range(PAIR_ROWS):
                    group, k = divmod(local, 2 * TOPK)
                    parity, t = divmod(group, TT)
                    table = peer_u if k < TOPK else peer_v
                    slot, c = local % ROWS, t * TOPK + k % TOPK
                    if k in (0, TOPK // 2):
                        pool.wait_ge(s_idx, i * 4 * TT + 2 * (parity * TT + t) + k // (TOPK // 2) + 1)
                    pool.wait_ge(s_row_used, i * PAIR_ROWS + local + 1)
                    pool.wait_ge(s_hold, i * PAIR_ROWS + local + 1)
                    g.tensor_tensor(tick[:, slot:slot + 1], tick[:, ROWS:ROWS + 1], tick[:, ROWS:ROWS + 1],
                                    ALU.add).then_inc(s_hold, 1)
                    g.indirect_dma_start(ring_row(slot), None, table,
                                         bass.IndirectOffsetOnAxis(ap=idx[parity][:, c:c + 1], axis=0)
                                         ).then_inc(s_row[slot], 16)

        @block.tensor
        def _(pe):
            mm = nc.tensor.matmul

            def token_sums(dst, parts):
                for k, sq in enumerate(parts):
                    last = mm(dst[:, 0:TOK], ones[:, :], sq, start=(k == 0), stop=(k == len(parts) - 1))
                last.then_inc(s_stat, 1)

            def rows_of(columns_, banks, done):
                for k in range(KC):
                    last = mm(banks[k // 4][:, k % 4 * P:(k % 4 + 1) * P], columns_[:, k:k + 1].broadcast_to([P, P]),
                              ident[:, :], start=True, stop=True)
                    if k % 4 == 3:
                        last.then_inc(done, 1)

            def part_of_chunk(dst, weights, src, chunks_, ready=None, start=False, stop=False):
                for n, k in enumerate(chunks_):
                    if ready is not None:
                        pe.wait_ge(ready[0], ready[1] + n + 1)
                    last = mm(dst[:, 0:src.shape[-1]], weights[:, k * P:(k + 1) * P], src[:, k, :],
                              start=start and n == 0, stop=stop and n == len(chunks_) - 1)
                return last

            def weight_chunk(dst, weights, src, ready=None):
                part_of_chunk(dst, weights, src, range(KC), ready, start=True, stop=True).then_inc(s_w_used, 1)

            pe.wait_ge(s_ident, 1)
            pe.wait_ge(s_silu, 2)
            rows_of(silu_c, bank[0:4], s_silups)

            pe.wait_ge(s_ones, 1)
            pe.wait_ge(s_sq1, 4)
            token_sums(bank[STAT_BANK], [mixedT[:, k, :] for k in range(KC)])
            pe.wait_ge(s_silurow, 4)

            for k in range(KC):
                pe.wait_ge(s_w[k % WSLOTS], 16 * (k // WSLOTS + 1))
                pe.wait_ge(s_h, k + 1)
                for t in range(TT):
                    for dst, a, b in ((2 * t, 0, 512), (2 * t + 1, 512, 1024), (4 + t, 1024, QKV)):
                        last = mm(bank[dst][:, 0:b - a], hT[:, k, t * P:(t + 1) * P], w_ring[:, k % WSLOTS, a:b],
                                  start=(k == 0), stop=(k == KC - 1))
                last.then_inc(s_w_used, 1)

            def qk_transpose():
                pe.wait_ge(s_qk, TT)
                for t in range(TT):
                    for pair in range(8):
                        dst = (EVEN_BANK, ODD_BANK, PT_BANK, STAT_BANK)[2 * t + pair // 4]
                        nc.tensor.transpose(bank[dst][:, pair % 4 * P:(pair % 4 + 1) * P],
                                            qS[:, t, pair * P:(pair + 1) * P], ident[:, :])
                for kv in range(NKV):
                    for t in range(TT):
                        at_ = (kv * TT + t) * P
                        last = nc.tensor.transpose(bank[PV_BANK][:, at_:at_ + P],
                                                   kdup[:, t, kv, :, :].rearrange("p u d -> p (u d)"), ident[:, :])
                last.then_inc(s_qkTps, 1)

            def scores(u):
                t, heads, keys_n = unit_heads(u)
                pe.wait_ge(s_qkT, 5)
                if u:
                    pe.wait_ge(s_scS, 2 * u)
                for i, h in enumerate(heads):
                    o, at_ = h % 2, i % (len(heads) // 2) * keys_n
                    last = mm(bank[(EVEN_BANK, ODD_BANK)[o]][:, at_:at_ + keys_n],
                              qTr[o * HD:(o + 1) * HD, t, h // 2, :],
                              kTr[o * HD:(o + 1) * HD, h // (NQ // NKV), 0:keys_n], start=True, stop=True)
                last.then_inc(s_scps, 1)

            def transpose_probs(u):
                t, heads, keys_n = unit_heads(u)
                nb = keys_n // P
                pr = probs[u % 2][:, 0:len(heads) * (keys_n + 1)].rearrange("p (h k) -> p h k", h=len(heads))
                pe.wait_ge(s_prob, u + 1)
                for b in range(8):
                    if u and b % 4 == 0:
                        pe.wait_ge(s_PT, 2 * (u - 1) + b // 4 + 1)
                    last = nc.tensor.transpose(bank[(PT_BANK, STAT_BANK)[b // 4]][:, b % 4 * P:(b % 4 + 1) * P],
                                               pr[:, b // nb, b % nb * P:(b % nb + 1) * P], ident[:, :])
                    if b % 4 == 3:
                        last.then_inc(s_PTps, 1)

            def values(u):
                t, heads, keys_n = unit_heads(u)
                nb = keys_n // P
                pe.wait_ge(s_PT, 2 * u + 2)
                if u:
                    pe.wait_ge(s_pv, u)
                for i, h in enumerate(heads):
                    o, pair, kv = h % 2, (h - heads[0]) // 2, h // (NQ // NKV)
                    for b in range(nb):
                        last = mm(bank[PV_BANK][o * HD:(o + 1) * HD, pair * P:(pair + 1) * P],
                                  kvS[:, b, P + kv * HD:P + (kv + 1) * HD],
                                  probsT[u % 2][:, (i * nb + b) * P:(i * nb + b + 1) * P],
                                  start=(b == 0), stop=(b == nb - 1))
                last.then_inc(s_pvps, 1)

            def gates_of(c):
                if c == 0:
                    pe.wait_ge(s_gatew, 16)
                pe.wait_ge(s_conv, c + 1)
                if c:
                    pe.wait_ge(s_gev, 2 * c)
                for gate in range(2):
                    last = mm(bank[GATE_BANK][:, gate * TOK:(gate + 1) * TOK], gate_w[:, gate, c, :],
                              xconv[c % 2], start=True, stop=True)
                last.then_inc(s_gps, 1)

            for c in range(LC):
                u = c - FIRST_UNIT_CHUNK
                n = KC + 2 * c
                pe.wait_ge(s_w[n % WSLOTS], 16 * (n // WSLOTS + 1))
                if c:
                    pe.wait_ge(s_xev, c)
                else:
                    pe.wait_ge(s_qkvS, 1)
                weight_chunk(bank[X_BANK], w_ring[:, n % WSLOTS, :], hT)
                if c:
                    gates_of(c - 1)
                if u >= 0:
                    transpose_probs(u)
                n += 1
                pe.wait_ge(s_w[n % WSLOTS], 16 * (n // WSLOTS + 1))
                if c:
                    pe.wait_ge(s_yev, c)
                else:
                    pe.wait_ge(s_qkvS, 6)
                if c < LC - 1:
                    weight_chunk(bank[Y_BANK], w_ring[:, n % WSLOTS, :], hT)
                else:
                    part_of_chunk(bank[Y_BANK], w_ring[:, n % WSLOTS, :], hT, range(6), start=True)
                    gates_of(c)
                    part_of_chunk(bank[Y_BANK], w_ring[:, n % WSLOTS, :], hT, range(6, KC), stop=True
                                  ).then_inc(s_w_used, 1)
                if u >= 0:
                    values(u)
                if u == -1:
                    qk_transpose()
                if -1 <= u < UNITS - 1:
                    scores(u + 1)
            pe.wait_ge(s_attnsum, TT + pairs_before(UNITS - 1))
            pe.wait_ge(s_lastsq, 1)
            mm(bank[STAT_BANK][:, 0:TOK], ones[:, :], attn_sum[:, :], start=True, stop=False)
            for a in range(2):
                last = mm(bank[STAT_BANK][:, P:TOK], ones[:, :], last_sq[:, a * P:(a + 1) * P],
                          start=False, stop=(a == 1))
            last.then_inc(s_stat, 1)
            pe.wait_ge(s_lrusum, LC)
            pe.wait_ge(s_lastsq, 2)
            token_sums(bank[PT_BANK], [lru_sum[:, :], last_sq[:, TOK:2 * TOK]])

            attention, lru = MIX_ORDER[0:LC], MIX_ORDER[LC:]
            for j in range(2):
                pe.wait_ge(s_w[j], 16 * (2 * KC // WSLOTS + 1))
                part_of_chunk(bank[j], w_ring[:, j, :], mixedT, attention, (s_mix, 0) if j == 0 else None, start=True)
            for j in range(2):
                part_of_chunk(bank[j], w_ring[:, j, :], mixedT, lru, (s_mix, LC) if j == 0 else None, stop=True
                              ).then_inc(s_w_used, 1)
            for j in range(2, WSLOTS):
                pe.wait_ge(s_w[j], 16 * (2 * KC // WSLOTS + 1))
                weight_chunk(bank[j], w_ring[:, j, :], mixedT)
            with pe.Fori(1, KC // WSLOTS) as i:
                for j in range(WSLOTS):
                    pe.wait_ge(s_w[j], i * 16 + 16 * (2 * KC // WSLOTS + 1))
                    pe.wait_ge(s_x2, (i - 1) * WSLOTS + j + 1)
                    weight_chunk(bank[j], w_ring[:, j, :], mixedT)

            def peer_scores(head, turn, slot):
                for half in range(2):
                    if slot is None:
                        pe.wait_ge(s_wx[half], 16)
                        weights = ada_ring[:, half, :]
                    else:
                        pe.wait_ge(s_w[slot + half], turn * 16 + 16 * (3 * KC // WSLOTS + 1))
                        weights = w_ring[:, slot + half, :]
                    pe.wait_ge(s_qev, head * 2 + half - 1)
                    weight_chunk(bank[half], weights, hT)
                pe.wait_ge(s_bests, head * TT)
                for half in range(2):
                    pe.wait_ge(s_qev, head * 2 + half + 1)
                    last = scores_half(half, keysT[:, bass.ds(head * 2 + half, 1), :].rearrange("p a n -> p (a n)"))
                last.then_inc(s_sps, 1)

            def scores_half(half, kt):
                for t in range(TT):
                    at_ = (half * TT + t) * P
                    last = mm(bank[2][:, at_:at_ + P], qpT[half][:, t * P:(t + 1) * P], kt, start=True, stop=True)
                return last

            pe.wait_ge(s_w[0], 16 * (3 * KC // WSLOTS + 1))
            pe.wait_ge(s_shift2, 1)
            weight_chunk(bank[0], w_ring[:, 0, :], h_wide, (s_amp, 1))
            pe.wait_ge(s_x2add, WSLOTS + KC)
            token_sums(bank[STAT_BANK], [sqsum[:, :]])
            pe.wait_ge(s_w[1], 16 * (3 * KC // WSLOTS + 1))
            weight_chunk(bank[1], w_ring[:, 1, :], h_wide)
            pe.wait_ge(s_keys, 16)
            for half in range(2):
                pe.wait_ge(s_qev, half + 1)
                last = scores_half(half, keysT[:, half, :])
            last.then_inc(s_sps, 1)
            for n in range(TT * 4):
                t, quarter = divmod(n, 4)
                dst = bank[(3, 4, 5, 7)[n % 4]]
                if n >= 4:
                    pe.wait_ge(s_h2tok, n - 3)
                if t == 0:
                    pe.wait_ge(s_h2, 4 * n + 4)
                for k in range(4):
                    last = nc.tensor.transpose(dst[:, k * P:(k + 1) * P],
                                               hT[:, quarter * 4 + k, t * P:(t + 1) * P], ident[:, :])
                last.then_inc(s_h2ps, 1)
            pe.wait_ge(s_h2tok, TT * 4)
            peer_scores(1, 0, 2)
            peer_scores(2, 0, None)
            with pe.Fori(1, 3) as i:
                for parity in range(2):
                    peer_scores(i * 2 + 1 + parity, i, 2 * parity)
            peer_scores(PH - 1, 3, 0)

            pe.wait_ge(s_bests, PH * TT)
            for t in range(TT):
                if t:
                    pe.wait_ge(s_adacol, 4)
                    rows_of(ada_col[:, G2, :], bank[3:7], s_g2ps)
                    pe.wait_ge(s_g2, 4)
                for n in range(4):
                    dst = bank[((0, 1, 2, 7), (3, 4, 5, 6))[t][n]]
                    for k in range(4):
                        last = nc.tensor.transpose(dst[:, k * P:(k + 1) * P],
                                                   x2T[:, n * 4 + k, t * P:(t + 1) * P], ident[:, :])
                    last.then_inc(s_x2ps, 1)

        @block.scalar
        def _(act):
            fn = nc.scalar.activation
            own = Chain(act, s_act)
            act.wait_ge(s_cols, 16)
            fn(amp, col("c"), ACT.Tanh, scale=0.5).then_inc(s_silu, 1)
            own.mark(fn(lam_t[0], col("lam"), ACT.Abs))
            own.settle()
            fn(lam_t[0], lam_t[0], ACT.Exp, scale=-1.0).then_inc(s_lamexp, 1)
            act.wait_ge(s_xin, 16)
            for q in range(4):
                fn(mixedT[:, 4 * q:4 * q + 4, :], x2T[:, 4 * q:4 * q + 4, :], ACT.Square).then_inc(s_sq1, 1)
            act.wait_ge(s_ang, 1)
            fn(sin_t, angle, ACT.Sin).then_inc(s_sin, 1)
            fn(cos_t, angle, ACT.Sin, scale=0.5).then_inc(s_sin, 1)

            roots = [0]

            def root(v):
                roots[0] += 1
                act.wait_ge(s_mean, roots[0])
                fn(v, v, ACT.Sqrt).then_inc(s_root, 1)

            root(rinv[:, :])
            for k in range(KC):
                act.wait_ge(s_scaled, k + 1)
                act.wait_ge(s_shift1, k + 1)
                act.wait_ge(s_scale1, k + 1)
                fn(hT[:, k, :], hT[:, k, :], ACT.Identity, bias=ada_col[:, SH1, k:k + 1], scale=amp[:, k:k + 1]
                   ).then_inc(s_h, 1)

            act.wait_ge(s_w_used, KC)
            for t in range(TT):
                for b, dst in ((2 * t, qS[:, t, 0:512]), (2 * t + 1, qS[:, t, 512:1024]), (4 + t, kvS[:, t, :])):
                    fn(dst, bank[b][:, 0:dst.shape[-1]], ACT.Copy).then_inc(s_qkvS, 1)

            def qk_transpose():
                act.wait_ge(s_qkTps, 1)
                for n, b in enumerate((EVEN_BANK, ODD_BANK, PT_BANK, STAT_BANK)):
                    fn(qTr[:, n // 2, n % 2 * 4:n % 2 * 4 + 4, :], bank[b][:, :].rearrange("p (h n) -> p h n", h=4),
                       ACT.Copy).then_inc(s_qkT, 1)
                fn(kTr, bank[PV_BANK][:, :].rearrange("p (k n) -> p k n", k=NKV), ACT.Copy).then_inc(s_qkT, 1)

            def qk_root(t):
                act.wait_ge(s_qkms, t + 1)
                fn(qk_ms, qk_ms, ACT.Sqrt).then_inc(s_qkroot, 1)

            def scores(u):
                _, heads, keys_n = unit_heads(u)
                act.wait_ge(s_shift, u + 1)
                v = probs[u % 2][:, 0:len(heads) * (keys_n + 1)].rearrange("p (h k) -> p h k", h=len(heads))
                for h in range(len(heads)):
                    fn(v[:, h, :], v[:, h, :], ACT.Exp, bias=neg_max[:, h:h + 1], accum_out=den[:, h:h + 1]
                       ).then_inc(s_exp, 1)

            def probs_out(u):
                for b in range(2):
                    act.wait_ge(s_PTps, 2 * u + b + 1)
                    if u >= 2 and b == 0:
                        act.wait_ge(s_pvps, u - 1)
                    fn(probsT[u % 2][:, b * 512:(b + 1) * 512], bank[(PT_BANK, STAT_BANK)[b]][:, :],
                       ACT.Copy).then_inc(s_PT, 1)

            def values_out(u):
                t, heads, _ = unit_heads(u)
                act.wait_ge(s_pvps, u + 1)
                pairs, first = len(heads) // 2, heads[0] // 2
                fn(mixedT[:, LC + first:LC + first + pairs, t * P:(t + 1) * P],
                   bank[PV_BANK][:, 0:pairs * P].rearrange("p (h n) -> p h n", h=pairs),
                   ACT.Copy).then_inc(s_pv, 1)

            def gates_of(c):
                b = c % 2
                if c == 0:
                    act.wait_ge(s_lam, 1)
                if c >= 2:
                    act.wait_ge(s_lru, c - 1)
                act.wait_ge(s_gps, c + 1)
                fn(th_r[b], bank[GATE_BANK][:, 0:TOK], ACT.Tanh, bias=half_ab[:, c:c + 1], scale=0.5
                   ).then_inc(s_gev, 1)
                fn(th_i[b], bank[GATE_BANK][:, TOK:2 * TOK], ACT.Tanh, bias=half_xb[:, c:c + 1], scale=0.5
                   ).then_inc(s_gev, 1)
                act.wait_ge(s_gev, 2 * c + 1)
                fn(decay[b], th_r[b], ACT.Exp, bias=c4[:, c:c + 1], scale=c4[:, c:c + 1]).then_inc(s_decay, 1)
                fn(drive[b], th_r[b], ACT.Tanh, bias=c4[:, c:c + 1], scale=c4[:, c:c + 1]).then_inc(s_decay, 1)

            def input_scale(c):
                act.wait_ge(s_mag, c + 1)
                fn(drive[c % 2], drive[c % 2], ACT.Sqrt, scale=-1.0).then_inc(s_sqrt, 1)

            for c in range(LC):
                b = c % 2
                u = c - FIRST_UNIT_CHUNK
                if c == 0:
                    qk_root(0)
                if u >= 0:
                    scores(u)
                act.wait_ge(s_w_used, KC + 2 * c + 1)
                if c >= 2:
                    act.wait_ge(s_conv, c - 1)
                elif c == 0:
                    act.wait_ge(s_const, 8)
                fn(xpad[b][:, 3:3 + TOK], bank[X_BANK][:, 0:TOK], ACT.Copy).then_inc(s_xev, 1)
                if c >= 2:
                    act.wait_ge(s_gps, c - 1)
                act.wait_ge(s_xev, c + 1)
                fn(xconv[b], xpad[b][:, 0:TOK], ACT.Identity, bias=col("conv_b", c), scale=col("conv_w", c)
                   ).then_inc(s_tap, 1)
                if c == 0:
                    qk_root(1)
                if c:
                    gates_of(c - 1)
                if u >= 0:
                    probs_out(u)
                if c:
                    input_scale(c - 1)
                if c == LC - 1:
                    gates_of(c)
                act.wait_ge(s_w_used, KC + 2 * c + 2)
                if c >= 2:
                    act.wait_ge(s_lru, c - 1)
                fn(ysil[b], bank[Y_BANK][:, 0:TOK], ACT.Gelu_apprx_tanh).then_inc(s_yev, 1)
                if u >= 0:
                    values_out(u)
                if u == -1:
                    qk_transpose()
            act.wait_ge(s_pv, UNITS)
            fn(last_sq[:, 0:TOK].rearrange("p (a b) -> p a b", a=2), mixedT[:, KC - 2:KC, P:TOK], ACT.Square
               ).then_inc(s_lastsq, 1)
            input_scale(LC - 1)
            root(sqsum[:, :])
            act.wait_ge(s_lru, LC)
            fn(last_sq[:, TOK:2 * TOK], mixedT[:, LC - 1, :], ACT.Square).then_inc(s_lastsq, 1)
            root(rinv[:, :])

            with act.Fori(0, KC // WSLOTS) as i:
                for j in range(WSLOTS):
                    act.wait_ge(s_x2, i * WSLOTS + j + 1)
                    act.wait_ge(s_x2add, i * WSLOTS + j + 1)
                    fn(x2_squares[:, j * TOK:(j + 1) * TOK].unsqueeze(1),
                       x2T[:, bass.ds(i * WSLOTS + j, 1), :], ACT.Square).then_inc(s_x2sq, 1)
            root(rinv[:, :])
            act.wait_ge(s_adacol, 3)
            for k in range(KC):
                act.wait_ge(s_scaled, KC + k + 1)
                fn(hT[:, k, :], hT[:, k, :], ACT.Identity, bias=ada_col[:, SH2, k:k + 1]).then_inc(s_h2, 1)

            def queries(head):
                for half in range(2):
                    act.wait_ge(s_w_used, head * 2 + half + 3 * KC + 1)
                    if half == 0:
                        act.wait_ge(s_sps, head)
                    fn(qpT[half][:, :], bank[half][:, 0:TOK], ACT.Copy).then_inc(s_qev, 1)

            def best_exp(head, t):
                act.wait_ge(s_bests, head * TT + t + 1)
                fn(best_e[:, t, :], best_e[:, t, :], ACT.Exp, accum_out=tksum[:, t:t + 1]).then_inc(s_bexp, 1)

            def expert_gelu(head, t):
                act.wait_ge(s_row_used, head * (2 * TT * TOPK) + t * 2 * TOPK + TOPK + ROWS)
                fn(gel, dots, ACT.Gelu_apprx_tanh).then_inc(s_gelu, 1)

            for n in range(TT * 4):
                t, quarter = divmod(n, 4)
                act.wait_ge(s_h2ps, n + 1)
                fn(h2tok[:, t, quarter * 512:(quarter + 1) * 512], bank[(3, 4, 5, 7)[n % 4]][:, :], ACT.Copy
                   ).then_inc(s_h2tok, 1)
            for t in range(TT):
                best_exp(0, t)
            def head_step(head, more):
                if more:
                    queries(head + 1)
                for t in range(TT):
                    expert_gelu(head, t)
                    if more:
                        best_exp(head + 1, t)
                    elif t == 0:
                        for n in range(4):
                            act.wait_ge(s_g2ps, n + 1)
                            fn(gate2[:, n * 512:(n + 1) * 512], bank[3 + n][:, :], ACT.Copy).then_inc(s_g2, 1)

            with act.Fori(0, PH - 1) as head:
                head_step(head, True)
            head_step(PH - 1, False)


        @block.vector
        def _(dve):
            v = nc.vector
            own = Chain(dve, s_dve)

            def link(ins):
                own.mark(ins)
                own.settle()

            dve.sem_inc(s_row_used, ROWS)
            v.memset(ones[:, :], 1.0).then_inc(s_ones, 1)
            for b in range(2):
                own.mark(v.memset(xpad[b][:, 0:3], 0.0))
            for j in range(ROT):
                own.mark(v.memset(invf[:, j:j + 1], float(np.float32(ROPE_THETA ** (-j / ROT)))))
            dve.wait_ge(s_cols, 16)
            dve.wait_ge(s_silu, 1)
            link(v.scalar_tensor_tensor(silu_c, amp, 1.0, col("c"), ALU.add, ALU.mult))
            v.tensor_scalar(silu_c, silu_c, 0.5, None, ALU.mult).then_inc(s_silu, 1)
            gained_bias = ada_col[:, SC1, :]
            link(v.scalar_tensor_tensor(gained_bias, col("b_ada")[:, SC1 * KC:(SC1 + 1) * KC], 1.0, col("norm1_g"),
                                        ALU.add, ALU.mult))
            for n in range(4):
                dve.wait_ge(s_silups, n + 1)
                v.tensor_copy(silu_row[:, n * 512:(n + 1) * 512], bank[n][:, :]).then_inc(s_silurow, 1)

            def ada_product(slot, dst):
                v.tensor_tensor_reduce(ada_ring[:, slot, :], ada_ring[:, slot, :], silu_row[:, :], 1.0, 0.0,
                                       ALU.mult, ALU.add, dst).then_inc(s_ada_used, 1)

            def ada_piece(n):
                g, k = divmod(n, KC)
                dve.wait_ge(s_ada[n % ASLOTS], 16 * (n // ASLOTS + 1))
                ada_product(n % ASLOTS, ada_col[:, g, k:k + 1])
                if k == KC - 1:
                    dve.wait_ge(s_ada_used, n + 1)
                    v.tensor_tensor(ada_col[:, g, :], ada_col[:, g, :], col("b_ada")[:, g * KC:(g + 1) * KC], ALU.add
                                    ).then_inc(s_adacol, 1)
                    dve.wait_ge(s_adacol, g - G1 + 1)

            means = [0]

            def mean(dst, src, n):
                means[0] += 1
                dve.wait_ge(s_stat, means[0])
                v.tensor_scalar(dst, src[:, 0:TOK], 1.0 / n, EPS, ALU.mult, ALU.add).then_inc(s_mean, 1)

            def invert(dst, n):
                dve.wait_ge(s_root, n)
                v.reciprocal(dst, dst).then_inc(s_inv, 1)
                dve.wait_ge(s_inv, n)

            def gain_and_scale(gain, g):
                v.scalar_tensor_tensor(amp, ada_col[:, g, :], 1.0, col(gain), ALU.add, ALU.mult).then_inc(s_amp, 1)

            dve.wait_ge(s_silurow, 4)
            dve.wait_ge(s_pos, 16)
            link(v.tensor_copy(posf, posi))
            for t in range(TT):
                own.mark(v.tensor_scalar(angle[:, t * ROT:(t + 1) * ROT], invf, posf[:, t:t + 1], None, ALU.mult))
            own.settle()
            link(v.tensor_scalar(turns, angle, 1.0 / (2 * math.pi), None, ALU.mult))
            magic = 1.5 * 2.0 ** 23
            link(v.tensor_scalar(turns, turns, magic, None, ALU.add))
            link(v.tensor_scalar(turns, turns, magic, None, ALU.subtract))
            rest = 2 * math.pi
            for bits in (6, 18, None):
                part_ = rest if bits is None else math.floor(rest * 2.0 ** bits) / 2.0 ** bits
                rest -= part_
                link(v.scalar_tensor_tensor(angle, turns, -float(np.float32(part_)), angle, ALU.mult, ALU.add))
            v.tensor_scalar(angle, angle, 3.1415925, -3.1415925, ALU.min, ALU.max).then_inc(s_ang, 1)

            dve.wait_ge(s_lamexp, 1)
            z, zz, s, b1 = lam_t
            link(v.tensor_scalar(zz, z, 2.0, None, ALU.add))
            link(v.reciprocal(zz, zz))
            link(v.tensor_tensor(z, z, zz, ALU.mult))
            link(v.tensor_tensor(zz, z, z, ALU.mult))
            link(v.tensor_scalar(s, zz, 1.0 / 17, None, ALU.mult))
            for odd in (15, 13, 11, 9, 7, 5, 3):
                link(v.scalar_tensor_tensor(s, s, 1.0 / odd, zz, ALU.add, ALU.mult))
            link(v.scalar_tensor_tensor(s, s, 1.0, z, ALU.add, ALU.mult))
            link(v.tensor_scalar(b1, col("lam"), -1.0, 0.0, ALU.mult, ALU.max))
            link(v.scalar_tensor_tensor(s, s, 2.0, b1, ALU.mult, ALU.add))
            own.mark(v.tensor_scalar(half_ab, col("gate_a_b"), 0.5, None, ALU.mult))
            own.mark(v.tensor_scalar(half_xb, col("gate_x_b"), 0.5, None, ALU.mult))
            own.settle()
            v.tensor_scalar(c4, s, -4.0, None, ALU.mult).then_inc(s_lam, 1)

            dve.wait_ge(s_sin, 2)
            link(v.tensor_tensor(cos_t, cos_t, cos_t, ALU.mult))
            link(v.tensor_scalar(cos_t, cos_t, -2.0, 1.0, ALU.mult, ALU.add))

            def part_at(k):
                return slice(k, k + 1) if isinstance(k, int) else bass.ds(k, 1)

            def shift1_scale1(i):
                for j in range(0, ASLOTS, 2):
                    for n in (j, j + 1):
                        dve.wait_ge(s_ada[n], i * 16 + 16)
                        ada_product(n, ada_dot[:, n:n + 1])
                    dve.wait_ge(s_ada_used, i * ASLOTS + j + 2)
                    k = part_at(i * 2 + j // 2)
                    v.tensor_scalar(ada_col[:, SH1, k], ada_dot[:, j:j + 1],
                                    col("b_ada")[:, part_at(i * 2 + j // 2 + SH1 * KC)], None, ALU.add
                                    ).then_inc(s_shift1, 1)
                    v.tensor_scalar(amp[:, k], ada_dot[:, j + 1:j + 2], col("norm1_g")[:, k], gained_bias[:, k],
                                    ALU.mult, ALU.add).then_inc(s_scale1, 1)

            shift1_scale1(0)
            mean(rinv[:, :], bank[STAT_BANK], D)
            invert(rinv[:, :], 1)
            with dve.Fori(1, KC // 2) as i:
                shift1_scale1(i)

            def qk_norm(t):
                dve.wait_ge(s_qkvS, 3 * (t + 1))
                dve.wait_ge(s_rows, 16)
                q = qS[:, t, :].rearrange("p (h d) -> p h d", h=NQ)
                k = kvS[:, t, 0:P].rearrange("p (h d) -> p h d", h=NKV)
                sq = qk_square.rearrange("p (h d) -> p h d", h=NQK)
                own.mark(v.tensor_tensor(sq[:, 0:NQ, :], q, q, ALU.mult))
                own.mark(v.tensor_tensor(sq[:, NQ:NQK, :], k, k, ALU.mult))
                own.settle()
                link(v.tensor_reduce(qk_ms, sq, AX, ALU.add))
                v.tensor_scalar(qk_ms, qk_ms, 1.0 / HD, EPS, ALU.mult, ALU.add).then_inc(s_qkms, 1)
                dve.wait_ge(s_qkroot, t + 1)
                link(v.reciprocal(qk_ms, qk_ms))
                sides = ((q, NQ, qk_ms[:, 0:NQ], q_gain), (k, NKV, qk_ms[:, NQ:NQK], k_gain))
                for x, n, r, _ in sides:
                    own.mark(v.tensor_tensor(x, x, spread(r, HD, 2), ALU.mult))
                own.settle()
                for x, n, _, gain in sides:
                    own.mark(v.tensor_tensor(x, x, spread(gain, n, 1), ALU.mult))
                own.settle()
                sin, cos = sin_t[:, t * ROT:(t + 1) * ROT], cos_t[:, t * ROT:(t + 1) * ROT]
                places = []
                for x, n, base in ((q, NQ, 0), (k, NKV, 4 * NQ * ROT)):
                    tmp = qk_square[:, base:base + 4 * n * ROT].rearrange("p (a h d) -> p a h d", a=4, h=n)
                    places.append((x, tmp))
                    for a, (half, w) in enumerate(((0, cos), (1, sin), (1, cos), (0, sin))):
                        own.mark(v.tensor_tensor(tmp[:, a], x[:, :, half * ROT:(half + 1) * ROT],
                                                 spread(w, n, 1), ALU.mult))
                own.settle()
                for x, tmp in places:
                    own.mark(v.tensor_tensor(x[:, :, 0:ROT], tmp[:, 0], tmp[:, 1], ALU.subtract))
                    own.mark(v.tensor_tensor(x[:, :, ROT:2 * ROT], tmp[:, 2], tmp[:, 3], ALU.add))
                own.settle()
                for u in range(2):
                    last = v.tensor_copy(kdup[:, t, :, u, :], k)
                    if u == 0:
                        own.mark(last)
                own.settle()
                last.then_inc(s_qk, 1)

            def softmax(u):
                t, heads, keys_n = unit_heads(u)
                n = len(heads)
                pr = probs[u % 2][:, 0:n * (keys_n + 1)].rearrange("p (h k) -> p h k", h=n)
                if u >= 2:
                    dve.wait_ge(s_PTps, 2 * (u - 1))
                for o in range(2):
                    own.mark(v.tensor_copy(pr[:, o * n // 2:(o + 1) * n // 2, keys_n:keys_n + 1],
                                           sink[:, heads[0] + o:heads[0] + n:2].unsqueeze(2)))
                dve.wait_ge(s_scps, u + 1)
                for o, b in enumerate((EVEN_BANK, ODD_BANK)):
                    v.scalar_tensor_tensor(pr[:, o * n // 2:(o + 1) * n // 2, 0:keys_n],
                                           bank[b][:, :].rearrange("p (h k) -> p h k", h=n // 2), HD ** -0.5,
                                           spread(mask[t], n // 2, 1), ALU.mult, ALU.add).then_inc(s_scS, 1)
                own.settle()
                dve.wait_ge(s_scS, 2 * u + 2)
                link(v.tensor_reduce(neg_max[:, 0:n], pr, AX, ALU.max))
                v.tensor_scalar(neg_max[:, 0:n], neg_max[:, 0:n], -1.0, None, ALU.mult).then_inc(s_shift, 1)
                mid_piece()
                dve.wait_ge(s_exp, 2 * pairs_before(u + 1))
                link(v.reciprocal(den[:, 0:n], den[:, 0:n]))
                v.tensor_tensor(pr[:, :, 0:keys_n], pr[:, :, 0:keys_n], spread(den[:, 0:n], keys_n, 2),
                                ALU.mult).then_inc(s_prob, 1)

            pieces = iter(range(2 * KC, ADA_GROUPS * KC))

            def mid_piece():
                for n in itertools.islice(pieces, 1):
                    ada_piece(n)

            def convolve(c):
                b = c % 2
                dve.wait_ge(s_tap, c + 1)
                taps = [colv[:, COLS["conv_w"][0] + k * LC + c:COLS["conv_w"][0] + k * LC + c + 1] for k in range(4)]
                for k in range(1, 4):
                    ins = v.scalar_tensor_tensor(xconv[b], xpad[b][:, k:k + TOK], taps[k], xconv[b],
                                                 ALU.mult, ALU.add)
                    if k < 3:
                        link(ins)
                ins.then_inc(s_conv, 1)

            def magnitude(c):
                b = c % 2
                dve.wait_ge(s_decay, 2 * c + 2)
                link(v.tensor_tensor(bscan, decay[b], decay[b], ALU.mult))
                v.scalar_tensor_tensor(drive[b], bscan, 1.0, drive[b], ALU.add, ALU.mult).then_inc(s_mag, 1)
                dve.wait_ge(s_mag, c + 1)
                link(v.scalar_tensor_tensor(bscan, th_i[b], 1.0, xconv[b], ALU.add, ALU.mult))

            def recurrence(c):
                b = c % 2
                dve.wait_ge(s_sqrt, c + 1)
                link(v.scalar_tensor_tensor(bscan, bscan, 0.5, drive[b], ALU.mult, ALU.mult))
                link(v.tensor_tensor_scan(mixedT[:, c, :], decay[b], bscan, 0.0, ALU.mult, ALU.add))
                dve.wait_ge(s_yev, c + 1)
                v.tensor_tensor(mixedT[:, c, :], mixedT[:, c, :], ysil[b], ALU.mult).then_inc(s_lru, 1)

            for c in range(LC):
                u = c - FIRST_UNIT_CHUNK
                if c == 0:
                    qk_norm(0)
                    mid_piece()
                elif c == FIRST_UNIT_CHUNK:
                    mid_piece()
                if u >= 0:
                    softmax(u)
                convolve(c)
                if c == 0:
                    mid_piece()
                    qk_norm(1)
                if c != FIRST_UNIT_CHUNK:
                    mid_piece()
                if c:
                    magnitude(c - 1)
                mid_piece()
                if c:
                    recurrence(c - 1)
                    mid_piece()
                if c == 1:
                    mid_piece()
            magnitude(LC - 1)
            mid_piece()
            mean(sqsum[:, :], bank[STAT_BANK], LRU)
            recurrence(LC - 1)
            invert(sqsum[:, :], 2)
            for k in MIX_ORDER:
                if k == 0:
                    mid_piece()
                    mid_piece()
                    mean(rinv[:, :], bank[PT_BANK], LRU)
                    invert(rinv[:, :], 3)
                v.scalar_tensor_tensor(mixedT[:, k, :], mixedT[:, k, :], col("out_g", k),
                                       (rinv if k < LC else sqsum)[:, :], ALU.mult, ALU.mult).then_inc(s_mix, 1)
            gain_and_scale("norm2_g", SC2)
            dve.wait_ge(s_amp, 1)
            for c in range(KC):
                dve.wait_ge(s_w_used, 2 * KC + c + 1)
                v.scalar_tensor_tensor(x2T[:, c, :], bank[c % WSLOTS][:, 0:TOK], ada_col[:, G1, c:c + 1],
                                       x2T[:, c, :], ALU.mult, ALU.add).then_inc(s_x2, 1)
                if c == KC // 2:
                    v.tensor_copy(h_wide[:, :, TOK:TOK + 1], ada_col[:, SH2, :].unsqueeze(2)).then_inc(s_shift2, 1)
                dve.wait_ge(s_x2, c + 1)
                v.tensor_scalar(hT[:, c, :], x2T[:, c, :], amp[:, c:c + 1], None, ALU.mult).then_inc(s_amp, 1)
                mid_piece()
                mid_piece()
            mean(rinv[:, :], bank[STAT_BANK], D)
            invert(rinv[:, :], 4)
            for half in range(2):
                dve.wait_ge(s_w_used, 3 * KC + half + 1)
                own.mark(v.tensor_copy(query_shift[:, half:half + 1], bank[half][:, TOK:TOK + 1]))
                link(v.tensor_tensor(qpT[half][:, :], bank[half][:, 0:TOK], rinv[:, :], ALU.mult))
                v.tensor_scalar(qpT[half][:, :], qpT[half][:, :], query_shift[:, half:half + 1], None, ALU.add
                                ).then_inc(s_qev, 1)

            def top16(values_, src, at_):
                for j in range(len(src)):
                    own.mark(v.max(values_[j][:, 0:8], src[j]))
                own.settle()
                for j in range(len(src)):
                    own.mark(v.max_index(at_[j][:, 0:8], values_[j][:, 0:8], src[j]))
                own.settle()
                for j in range(len(src)):
                    own.mark(v.match_replace(src[j], values_[j][:, 0:8], src[j], GONE))
                own.settle()
                for j in range(len(src)):
                    own.mark(v.max(values_[j][:, 8:16], src[j]))
                own.settle()
                for j in range(len(src)):
                    own.mark(v.max_index(at_[j][:, 8:16], values_[j][:, 8:16], src[j]))
                own.settle()

            def select(head, parity, t):
                if t == 0:
                    dve.wait_ge(s_sps, head + 1)
                    link(v.tensor_copy(sc_s, bank[2][:, :]))
                top16([top_v[:, a, t, :] for a in range(2)],
                      [sc_s[:, (a * TT + t) * NKEY:(a * TT + t + 1) * NKEY] for a in range(2)],
                      [top_i[:, a, t, :] for a in range(2)])
                own.mark(v.tensor_scalar(top_f[:, 0, t], top_i[:, 0, t], float(NKEY), None, ALU.mult))
                own.mark(v.tensor_copy(top_f[:, 1, t], top_i[:, 1, t]))
                own.settle()
                off = 0
                for i0, r, n in RECTS:
                    for dst, src in ((cand_s, top_v), (cand_i, top_f)):
                        own.mark(v.tensor_tensor(
                            dst[:, t, off:off + r * n].rearrange("p (r n) -> p r n", r=r),
                            spread(src[:, 0, t, i0:i0 + r], n, 2), spread(src[:, 1, t, 0:n], r, 1), ALU.add))
                    off += r * n
                own.settle()
                top16([best_v[:, t, :]], [cand_s[:, t, :]], [best_p[:, t, :]])
                v.tensor_tensor(best_e[:, t, :], best_v[:, t, :], best_v[:, t, 0:1].broadcast_to([P, TOPK]),
                                ALU.subtract).then_inc(s_bests, 1)
                link(v.tensor_copy(best_f[:, t, :], best_p[:, t, :]))
                for half in range(2):
                    n = TOPK // 2
                    ks = slice(half * n, (half + 1) * n)
                    link(v.tensor_tensor(hot[:, ks], spread(best_f[:, t, ks], NCAND, 2), spread(iota_c, n, 1),
                                         ALU.is_equal))
                    link(v.tensor_tensor(hot[:, ks], hot[:, ks], spread(cand_i[:, t, :], n, 1), ALU.mult))
                    if half == 0:
                        dve.wait_ge(s_bests, head * TT + t + 1)
                    link(v.tensor_reduce(best_v[:, t, ks], hot[:, ks], AX, ALU.add))
                    v.tensor_copy(idx[parity][:, t * TOPK + half * n:t * TOPK + (half + 1) * n], best_v[:, t, ks]
                                  ).then_inc(s_idx, 1)
                dve.wait_ge(s_bexp, head * TT + t + 1)
                link(v.reciprocal(tksum[:, t:t + 1], tksum[:, t:t + 1]))
                link(v.tensor_scalar(gsm[parity][:, t * TOPK:(t + 1) * TOPK], best_e[:, t, :], tksum[:, t:t + 1],
                                     None, ALU.mult))

            def experts(i, parity, t):
                base = (parity * TT + t) * 2 * TOPK
                for k in range(TOPK):
                    local = base + k
                    dve.wait_ge(s_row[local % ROWS], i * (16 * PAIR_ROWS // ROWS) + 16 * (local // ROWS + 1))
                    v.tensor_tensor_reduce(ring_row(local % ROWS), ring_row(local % ROWS), h2tok[:, t, :], 1.0, 0.0,
                                           ALU.mult, ALU.add, dots[:, k:k + 1]).then_inc(s_row_used, 1)
                dve.wait_ge(s_gelu, i * 2 * TT + parity * TT + t + 1)
                link(v.tensor_tensor(wgt, gel, gsm[parity][:, t * TOPK:(t + 1) * TOPK], ALU.mult))
                for k in range(TOPK):
                    local = base + TOPK + k
                    dve.wait_ge(s_row[local % ROWS], i * (16 * PAIR_ROWS // ROWS) + 16 * (local // ROWS + 1))
                    dve.wait_ge(s_row_used, i * PAIR_ROWS + local + ROWS)
                    v.scalar_tensor_tensor(peer[:, t, :], ring_row(local % ROWS), wgt[:, k:k + 1], peer[:, t, :],
                                           ALU.mult, ALU.add).then_inc(s_row_used, 1)

            def head_pair(i, more):
                experts(i, 0, 0)
                select(i * 2 + 1, 1, 0)
                experts(i, 0, 1)
                select(i * 2 + 1, 1, 1)
                experts(i, 1, 0)
                if more:
                    select(i * 2 + 2, 0, 0)
                else:
                    finish(0)
                experts(i, 1, 1)
                if more:
                    select(i * 2 + 2, 0, 1)

            def finish(t):
                dve.wait_ge(s_g2, 4)
                dve.wait_ge(s_row_used, ROWS + PH * TT * 2 * TOPK - (TT - 1 - t) * 2 * TOPK)
                for n in range(4):
                    cols_ = slice(n * 512, (n + 1) * 512)
                    link(v.tensor_tensor(peer[:, t, cols_], peer[:, t, cols_], gate2[:, cols_], ALU.mult))
                    dve.wait_ge(s_x2ps, 4 * t + n + 1)
                    v.tensor_tensor(peer[:, t, cols_], peer[:, t, cols_],
                                    bank[((0, 1, 2, 7), (3, 4, 5, 6))[t][n]][:, :], ALU.add).then_inc(s_fin, 1)

            dve.wait_ge(s_const, 9)
            for t in range(TT):
                select(0, 0, t)
            dve.wait_ge(s_h2tok, TT * 4)
            own.restart()
            with dve.Fori(0, PH // 2 - 1) as i:
                head_pair(i, True)
                own.restart()
            head_pair(PH // 2 - 1, False)
            finish(1)


def kernel(**inputs):
    import concourse.bacc as bacc
    from concourse.bass_utils import run_bass_kernel_spmd

    a = {n: np.asarray(x) for n, x in inputs.items()}

    def columns(v):
        return v.reshape(-1, P).T

    w_in = a["w_in"][0]
    halves = w_in[:, 0:2 * LRU].reshape(KC, P, 2, LC, P)

    ada = a["w_ada"][0].T.reshape(ADA_GROUPS, KC, P, D)

    def chunks(w):
        return w.reshape(KC, P, -1, P).transpose(2, 1, 0, 3).reshape(-1, P, D)

    arrays = {
        "xT": a["x"][0].T.reshape(KC, P, TOK).transpose(1, 0, 2).reshape(P, KC * TOK),
        "cols": np.concatenate([columns(a["c"][0])]
                               + [columns(a["b_ada"][0].reshape(ADA_GROUPS, D)[g]) for g in ADA_PARTS]
                               + [columns(a[n][0]) for n in ("norm1_g", "norm2_g")]
                               + [columns(a["out_norm_lru_g"][0]), columns(a["out_norm_attn_g"][0])]
                               + [columns(a[n][0]) for n in ("conv_w", "conv_b", "lru_gate_a_b", "lru_gate_x_b",
                                                             "lru_lambda")], axis=1),
        "rowv": np.broadcast_to(np.concatenate([a["q_norm_g"][0], a["k_norm_g"][0], a["attn_sinks"][0]]), (P, NROWV)),
        "pos": a["positions"][0].reshape(TT, P).T,
        "w_ada": np.concatenate([ada[0:2].transpose(1, 0, 2, 3).reshape(2 * KC, P, D)]
                                + [ada[g] for g in ADA_PARTS[2:]]),
        "w_qkv": w_in[:, 2 * LRU:].reshape(KC, P, QKV),
        "w_chunks": np.concatenate([halves.transpose(3, 2, 1, 0, 4).reshape(KC, P, D), chunks(a["w_out"][0]),
                                    chunks(a["peer_w_q"][0])]),
        "gates": np.stack([a["lru_gate_a_w"][0], a["lru_gate_x_w"][0]]).transpose(2, 0, 1, 3).reshape(P, 2 * LC * P),
        "keys": a["peer_sub_keys"][0].transpose(3, 0, 1, 2).reshape(P, 2 * PH * NKEY),
        "peer_u": a["peer_u"][0],
        "peer_v": a["peer_v"][0],
    }
    nc = bacc.Bacc("TRN2", target_bir_lowering=False, num_devices=1)
    sent, args = {}, []
    for name, x in arrays.items():
        x = np.ascontiguousarray(x)
        sent[f"in_{name}"] = x
        args.append(nc.dram_tensor(f"in_{name}", x.shape, mybir.dt.from_np(x.dtype), kind="ExternalInput").ap())
    result = nc.dram_tensor("result", (TOK, D), F32, kind="ExternalOutput").ap()
    build(nc, *args, result)
    r = run_bass_kernel_spmd(nc, [sent], core_ids=[0])
    return r.results[0]["result"].reshape(1, TOK, D)
```
